# Optimizing a Trainium2 kernel written in Bass

```python
import math
import jax, jax.numpy as jnp
from jax import lax
import numpy as np

D_MODEL = 1024
BATCH = 1
SEQ = 512
DEPTH = 1

N_MIXERS = 2
N_ATTN_LAYERS = (DEPTH + N_MIXERS - 1) // N_MIXERS
N_SSM_LAYERS = DEPTH // N_MIXERS
DILATION_PAIRS = ((128, 1), (512, 4), (2048, 16))
N_GROUPS = len(DILATION_PAIRS)
HEADS_PER_GROUP = 8
HEAD_DIM = 128
ROPE_THETA = 10000.0
ATTN_IN_WIDTH = N_GROUPS * 3 * HEADS_PER_GROUP * HEAD_DIM
ATTN_OUT_WIDTH = HEADS_PER_GROUP * HEAD_DIM
D_SSM = D_MODEL
SSM_GROUP_CH = 16
SSM_GROUPS = D_SSM // SSM_GROUP_CH
SSM_STATE = 64
D_FF = 2816
CONV_WIDTH = 3
DEEPNORM_ALPHA = (2.0 * DEPTH) ** 0.25
DEEPNORM_BETA = (8.0 * DEPTH) ** -0.25
LN_EPS = 1e-5
NEG_INF = -1e30

kernel_name = "hybrid_dilated_attn_s5_convffn_deepnorm"

def layer_norm(x, g, b):
    xf = x.astype(jnp.float32)
    mu = jnp.mean(xf, axis=-1, keepdims=True)
    var = jnp.mean(jnp.square(xf - mu), axis=-1, keepdims=True)
    y = (xf - mu) * lax.rsqrt(var + LN_EPS) * g.astype(jnp.float32) + b.astype(jnp.float32)
    return y.astype(x.dtype)

def rotary(t, cos, sin):
    t1, t2 = jnp.split(t, 2, axis=-1)
    return jnp.concatenate([t1 * cos - t2 * sin, t2 * cos + t1 * sin], axis=-1)

def dilated_window_group(q, k, v, window, dilation):
    B_, S_, H, E = q.shape
    steps = window // dilation
    blk = steps
    chunk = dilation * blk
    s_pad = -(-S_ // chunk) * chunk
    nb = s_pad // chunk
    L = s_pad // dilation

    def to_blocks(t):
        t = jnp.pad(t, ((0, 0), (0, s_pad - S_), (0, 0), (0, 0)))
        t = t.reshape(B_, L, dilation, H, E).transpose(0, 2, 1, 3, 4)
        return t.reshape(B_, dilation, nb, blk, H, E)

    def with_prev(t):
        prev = jnp.pad(t[:, :, :-1], ((0, 0), (0, 0), (1, 0), (0, 0), (0, 0), (0, 0)))
        return jnp.concatenate([prev, t], axis=3)

    qb = to_blocks(q)
    kk = with_prev(to_blocks(k))
    vv = with_prev(to_blocks(v))
    scores = jnp.einsum('bdnqhe,bdnkhe->bdnhqk', qb, kk,
                        preferred_element_type=jnp.float32)
    qi = jnp.arange(blk)[:, None]
    kj = jnp.arange(2 * blk)[None, :]
    rel = qi + blk - kj
    band = (rel >= 0) & (rel <= steps)
    first = (jnp.arange(nb)[:, None, None] == 0) & (kj[None] < blk)
    valid = (band[None] & ~first)[None, None, :, None]
    scores = jnp.where(valid, scores, NEG_INF)
    m = jnp.max(scores, axis=-1, keepdims=True)
    p = jnp.exp(scores - m)
    l = jnp.sum(p, axis=-1, keepdims=True)
    o = jnp.einsum('bdnhqk,bdnkhe->bdnqhe', p, vv.astype(jnp.float32))
    o = o / l.transpose(0, 1, 2, 4, 3, 5)
    lse = (m + jnp.log(l))[..., 0].transpose(0, 1, 2, 4, 3)
    o = o.reshape(B_, dilation, L, H, E).transpose(0, 2, 1, 3, 4).reshape(B_, s_pad, H, E)[:, :S_]
    lse = lse.reshape(B_, dilation, L, H).transpose(0, 2, 1, 3).reshape(B_, s_pad, H)[:, :S_]
    return o, lse

def dilated_attention(h, w_in, w_out):
    B_, S_, _ = h.shape
    qkv = (h @ w_in).reshape(B_, S_, N_GROUPS, 3, HEADS_PER_GROUP, HEAD_DIM)
    pos = jnp.arange(S_, dtype=jnp.float32)
    inv_freq = ROPE_THETA ** (-jnp.arange(0, HEAD_DIM, 2, dtype=jnp.float32) / HEAD_DIM)
    ang = pos[:, None] * inv_freq[None, :]
    cos = jnp.cos(ang)[None, :, None, None, :].astype(h.dtype)
    sin = jnp.sin(ang)[None, :, None, None, :].astype(h.dtype)
    q = rotary(qkv[:, :, :, 0], cos, sin) * (HEAD_DIM ** -0.5)
    k = rotary(qkv[:, :, :, 1], cos, sin)
    v = qkv[:, :, :, 2]
    outs, lses = [], []
    for g, (window, dilation) in enumerate(DILATION_PAIRS):
        o, lse = dilated_window_group(q[:, :, g], k[:, :, g], v[:, :, g], window, dilation)
        outs.append(o)
        lses.append(lse)
    w = jax.nn.softmax(jnp.stack(lses, axis=0), axis=0)
    o = jnp.sum(w[..., None] * jnp.stack(outs, axis=0), axis=0)
    return o.reshape(B_, S_, ATTN_OUT_WIDTH).astype(h.dtype) @ w_out

def _ssm_combine(e1, e2):
    a1r, a1i, b1r, b1i = e1
    a2r, a2i, b2r, b2i = e2
    return (a2r * a1r - a2i * a1i,
            a2r * a1i + a2i * a1r,
            a2r * b1r - a2i * b1i + b2r,
            a2r * b1i + a2i * b1r + b2i)

def s5_mixer(h, w_in, a_re, a_im, log_dt, b_re, b_im, c_re, c_im, d_skip, w_glu, b_glu, w_out):
    f32 = jnp.float32
    B_, S_, _ = h.shape
    u = (h @ w_in).astype(f32)
    ug = u.reshape(B_, S_, SSM_GROUPS, SSM_GROUP_CH)
    a_re = a_re.astype(f32)
    a_im = a_im.astype(f32)
    dt = jnp.exp(log_dt.astype(f32))[:, None]
    mag = jnp.exp(a_re * dt)
    lam_re = mag * jnp.cos(a_im * dt)
    lam_im = mag * jnp.sin(a_im * dt)
    nr, ni = lam_re - 1.0, lam_im
    den = a_re * a_re + a_im * a_im
    coef_re = ((nr * a_re + ni * a_im) / den)[..., None]
    coef_im = ((ni * a_re - nr * a_im) / den)[..., None]
    b_re = b_re.astype(f32)
    b_im = b_im.astype(f32)
    bb_re = coef_re * b_re - coef_im * b_im
    bb_im = coef_re * b_im + coef_im * b_re
    bu_re = jnp.einsum('bsgc,gnc->bsgn', ug, bb_re)
    bu_im = jnp.einsum('bsgc,gnc->bsgn', ug, bb_im)
    lr = jnp.broadcast_to(lam_re, (1, S_, SSM_GROUPS, SSM_STATE))
    li = jnp.broadcast_to(lam_im, (1, S_, SSM_GROUPS, SSM_STATE))
    _, _, xr, xi = lax.associative_scan(_ssm_combine, (lr, li, bu_re, bu_im), axis=1)
    y = (jnp.einsum('bsgn,gcn->bsgc', xr, c_re.astype(f32))
         - jnp.einsum('bsgn,gcn->bsgc', xi, c_im.astype(f32)))
    y = y.reshape(B_, S_, D_SSM) + d_skip.astype(f32) * u
    z = jax.nn.gelu(y)
    z = z * jax.nn.sigmoid(z @ w_glu.astype(f32) + b_glu.astype(f32))
    return z.astype(h.dtype) @ w_out

def conv_ffn(h, w_up, conv_w, conv_b, w_down):
    S_ = h.shape[1]
    gate, val = jnp.split(h @ w_up, 2, axis=-1)
    gp = jnp.pad(gate, ((0, 0), (CONV_WIDTH - 1, 0), (0, 0)))
    conv = conv_b
    for t in range(CONV_WIDTH):
        conv = conv + conv_w[t] * gp[:, t:t + S_]
    return (jax.nn.silu(conv) * val) @ w_down

def setup_inputs(seed: int = 0) -> dict:
    key = jax.random.key(seed)
    ks = jax.random.split(key, 20)
    f32 = jnp.float32

    def nrm(k, shape, scale):
        return jax.random.normal(k, shape, f32) * scale

    nA, nB = N_ATTN_LAYERS, N_SSM_LAYERS
    G, N, C = SSM_GROUPS, SSM_STATE, SSM_GROUP_CH
    n_idx = jnp.arange(N, dtype=f32)
    return {
        "x": nrm(ks[0], (BATCH, SEQ, D_MODEL), 1.0),
        "attn_w_in": nrm(ks[1], (nA, D_MODEL, ATTN_IN_WIDTH), D_MODEL ** -0.5),
        "attn_w_out": nrm(ks[2], (nA, ATTN_OUT_WIDTH, D_MODEL), ATTN_OUT_WIDTH ** -0.5 * DEEPNORM_BETA),
        "ssm_w_in": nrm(ks[3], (nB, D_MODEL, D_SSM), D_MODEL ** -0.5),
        "ssm_a_re": -0.5 + nrm(ks[4], (nB, G, N), 0.01),
        "ssm_a_im": jnp.tile((math.pi * n_idx)[None, None, :], (nB, G, 1)),
        "ssm_log_dt": jax.random.uniform(ks[5], (nB, G), f32, math.log(1e-3), math.log(1e-1)),
        "ssm_b_re": nrm(ks[6], (nB, G, N, C), (2.0 * C) ** -0.5),
        "ssm_b_im": nrm(ks[7], (nB, G, N, C), (2.0 * C) ** -0.5),
        "ssm_c_re": nrm(ks[8], (nB, G, C, N), N ** -0.5),
        "ssm_c_im": nrm(ks[9], (nB, G, C, N), N ** -0.5),
        "ssm_d": nrm(ks[10], (nB, D_SSM), 1.0),
        "ssm_w_glu": nrm(ks[11], (nB, D_SSM, D_SSM), D_SSM ** -0.5),
        "ssm_b_glu": nrm(ks[12], (nB, D_SSM), 0.02),
        "ssm_w_out": nrm(ks[13], (nB, D_SSM, D_MODEL), D_SSM ** -0.5 * DEEPNORM_BETA),
        "ffn_w_up": nrm(ks[14], (DEPTH, D_MODEL, 2 * D_FF), D_MODEL ** -0.5),
        "ffn_conv_w": nrm(ks[15], (DEPTH, CONV_WIDTH, D_FF), CONV_WIDTH ** -0.5),
        "ffn_conv_b": nrm(ks[16], (DEPTH, D_FF), 0.02),
        "ffn_w_down": nrm(ks[17], (DEPTH, D_FF, D_MODEL), D_FF ** -0.5 * DEEPNORM_BETA),
        "ln_g": 1.0 + nrm(ks[18], (DEPTH, 2, D_MODEL), 0.02),
        "ln_b": nrm(ks[19], (DEPTH, 2, D_MODEL), 0.02),
    }

def reference(x, attn_w_in, attn_w_out, ssm_w_in, ssm_a_re, ssm_a_im, ssm_log_dt,
              ssm_b_re, ssm_b_im, ssm_c_re, ssm_c_im, ssm_d, ssm_w_glu, ssm_b_glu,
              ssm_w_out, ffn_w_up, ffn_conv_w, ffn_conv_b, ffn_w_down, ln_g, ln_b):
    for i in range(DEPTH):
        j = i // N_MIXERS
        if i % N_MIXERS == 0:
            y = dilated_attention(x, attn_w_in[j], attn_w_out[j])
        else:
            y = s5_mixer(x, ssm_w_in[j], ssm_a_re[j], ssm_a_im[j], ssm_log_dt[j],
                         ssm_b_re[j], ssm_b_im[j], ssm_c_re[j], ssm_c_im[j], ssm_d[j],
                         ssm_w_glu[j], ssm_b_glu[j], ssm_w_out[j])
        x = layer_norm(DEEPNORM_ALPHA * x + y, ln_g[i, 0], ln_b[i, 0])
        f = conv_ffn(x, ffn_w_up[i], ffn_conv_w[i], ffn_conv_b[i], ffn_w_down[i])
        x = layer_norm(DEEPNORM_ALPHA * x + f, ln_g[i, 1], ln_b[i, 1])
    return x


_drawn_inputs = setup_inputs


def setup_inputs(seed=0):
    import zlib

    import numpy as np

    out = dict(_drawn_inputs(seed))
    spreads = {}
    factors = {'ffn_conv_b': 8.0}
    for name, (base, spread) in spreads.items():
        noise = np.random.default_rng([zlib.crc32(name.encode()), seed]).standard_normal(out[name].shape)
        drawn = base * np.exp(spread * noise) if base else spread * noise
        out[name] = __import__('jax').numpy.asarray(drawn.astype(out[name].dtype))
    for name, factor in factors.items():
        out[name] = (out[name] * factor).astype(out[name].dtype)
    return out
```

```python
import math
from contextlib import ExitStack

import numpy as np

import concourse.bass as bass
from concourse import mybir

F32 = mybir.dt.float32
F32R = mybir.dt.float32r
ALU = mybir.AluOpType
ACT = mybir.ActivationFunctionType
X = mybir.AxisListType.X

P = 128
S = 512
D = 1024
KT = D // P
NR = 4
G = 3
H = 8
E = 128
PAIRS = H // 2
FF = 2816
FT = FF // P
CONV = 3
CW = 256
ALPHA = 2.0 ** 0.25
EPS = 1e-5
LN_STEPS = 6
SCALE = E ** -0.5
NEG = -1e30

CHUNKS = [(g, j) for g in range(G) for j in (0, 1)] + [(g, 2) for g in range(G)]
NC = len(CHUNKS)
QT = 12
VT = 12
OUT_CHUNKS = 4
QKV_CHUNKS = PAIRS * NC
UP0 = QKV_CHUNKS + OUT_CHUNKS
UP_STEPS = FT // 2
DOWN0 = UP0 + 2 * UP_STEPS
DOWN = FT // 2
DOWN_LOOP = 6
DOWN_TAIL = 7

C_COS, C_SIN, C_MASK, C_REP, C_SEL = 0, S, 2 * S, 2 * S + 512, 2 * S + 1536
C_ALL = C_SEL + 2 * NR


def constants():
    pos = np.arange(S, dtype=np.float32)
    inv = (np.float32(10000.0) ** (-np.arange(0, E, 2, dtype=np.float32) / np.float32(E))).astype(np.float32)
    ang = (inv[:, None] * pos[None, :]).astype(np.float32)
    out = np.zeros((P, C_ALL), np.float32)
    out[:64, C_COS:C_COS + S] = out[64:, C_COS:C_COS + S] = np.cos(ang.astype(np.float64))
    sin = np.sin(ang.astype(np.float64))
    out[:64, C_SIN:C_SIN + S], out[64:, C_SIN:C_SIN + S] = sin, -sin
    q, k = np.arange(P)[:, None], np.arange(P)[None, :]
    mask = np.full((P, 2, CW), NEG, np.float32)
    mask[:, 0, :P][k >= q] = 0
    mask[:, 0, P:][k <= q] = 0
    mask[:, 1, :P][k <= q] = 0
    mask[:, 1, P:][(k <= q) & ((q - k) % 4 == 0)] = 0
    out[:, C_MASK:C_MASK + 512] = mask.reshape(P, 512)
    rep, sel = np.zeros((P, 2, NR, P), np.float32), np.zeros((P, 2, NR), np.float32)
    p = np.arange(P)
    for t in range(NR):
        rep[32 * t + p // 4, 0, t, p] = 1
        rep[4 * (p % 32) + t, 1, t, p] = 1
    sel[p, 0, p % 4] = 1
    sel[p, 1, p // 32] = 1
    out[:, C_REP:C_REP + 1024] = rep.reshape(P, 1024)
    out[:, C_SEL:C_SEL + 8] = sel.reshape(P, 8)
    return out


def layer(nc, x, w_in, w_out, w_up, conv_w, conv_b, w_down, ln_g, ln_b, ident_in, const_in, out):
    es = ExitStack()
    with es:
        def sb(name, shape, dt=F32, scope=es):
            return scope.enter_context(nc.sbuf_tensor(name, shape, dt))

        def sem(name):
            return es.enter_context(nc.semaphore(name))

        raw = sb("raw", [P, 3, KT * CW])
        wh = [sb(f"wh{s}", [P, KT * CW], F32R) for s in range(3)]
        wl = [sb(f"wl{s}", [P, KT * CW], F32R) for s in range(3)]
        xTh = sb("xTh", [P, KT, S], F32R)
        xTl = sb("xTl", [P, KT, S], F32R)
        ident = sb("ident", [P, P])
        convp = sb("convp", [P, 4 * FT])
        small = sb("small", [P, 64])
        with ExitStack() as s0:
            x_rows = sb("x_rows", [P, NR, D], scope=s0)
            conv_rows = sb("conv_rows", [4 * FT, P], scope=s0)
        with ExitStack() as s1:
            qk = sb("qk", [P, 2, 2, 2, S], scope=s1)
            v = sb("v", [P, G, NR, CW], scope=s1)
            prob = sb("prob", [P, 4, NR, CW], scope=s1)
            probT = sb("probT", [P, 2, 8 * P], scope=s1)
            swapped = sb("swapped", [P, 2, S], scope=s1)
            oTh = sb("oTh", [P, H, S], F32R, scope=s1)
            oTl = sb("oTl", [P, H, S], F32R, scope=s1)
            const = sb("const", [P, C_ALL], scope=s1)
            stats = sb("stats", [P, 2, 2, 2, 8], scope=s1)
            picked = sb("picked", [P, 32, NR], scope=s1)
            merge = sb("merge", [P, 5, 2, 8], scope=s1)
            coef = sb("coef", [P, 2, 8], scope=s1)
            mweight = sb("mweight", [P, 2, 2, 8], scope=s1)
        with ExitStack() as s2:
            res = sb("res", [P, NR, D], scope=s2)
            lnp = sb("lnp", [P, 2, D], scope=s2)
            zrow = sb("zrow", [P, D], scope=s2)
            wh.append(sb("wh3", [P, KT * CW], F32R, scope=s2))
            wl.append(sb("wl3", [P, KT * CW], F32R, scope=s2))
            hidden = sb("hidden", [P, FT, S], scope=s2)
            cv = sb("cv", [P, 2, S], scope=s2)
            act = sb("act", [P, 2, S], scope=s2)
        bank = es.enter_context(nc.psum_tensor("bank", [P, 8, S], F32))
        OB, SB = 3, 4

        cosT, sinT = const[:, C_COS:C_COS + S], const[:, C_SIN:C_SIN + S]
        maskT = const[:, C_MASK:C_MASK + 512].rearrange("p (s k) -> p s k", s=2)
        repT = const[:, C_REP:C_REP + 1024].rearrange("p (s r k) -> p s r k", s=2, r=NR)
        selT = const[:, C_SEL:C_SEL + 8].rearrange("p (s o t) -> p s o t", s=2, o=1)

        ident_in_s, const_in_s, conv_in_s = sem("ident_loaded"), sem("const_loaded"), sem("conv_loaded")
        x_in_s = [sem(f"x_loaded{q}") for q in range(4)]
        raw_in = [sem(f"raw_loaded{s}") for s in range(3)]
        ff_in = [sem(f"ff_loaded{s}") for s in range(2)]
        high_ready, low_ready = sem("high_ready"), sem("low_ready")
        out_used, down_used = sem("out_used"), sem("down_used")
        x_turned, xh_ready, xl_ready = sem("x_turned"), sem("xh_ready"), sem("xl_ready")
        conv_turned, conv_ready = sem("conv_turned"), sem("conv_ready")
        qk_tile, v_tile = sem("qk_tile"), sem("v_tile")
        rope_terms, rotated = sem("rope_terms"), sem("rotated")
        v_stored = sem("v_stored")
        scores_ready, masked, shift_ready = sem("scores_ready"), sem("masked"), sem("shift_ready")
        probs_ready, stats_sent, merge_step = sem("probs_ready"), sem("stats_sent"), sem("merge_step")
        mweight_ready, coef_ready, scaled = sem("mweight_ready"), sem("coef_ready"), sem("scaled")
        turned, turned_act, turned_dve = sem("turned"), sem("turned_act"), sem("turned_dve")
        summed, head_high, head_low = sem("summed"), sem("head_high"), sem("head_low")
        res_in, ln_in = sem("res_loaded"), sem("ln_loaded")
        y_ready, ln_step, normed, scaled_g, ln_done = sem("y_ready"), sem("ln_step"), sem("normed"), sem("scaled_g"), sem("ln_done")
        x1_turned, x1h_ready, x1l_ready = sem("x1_turned"), sem("x1h_ready"), sem("x1l_ready")
        gate_ready, tap2, tap1, tap0 = sem("gate_ready"), sem("tap2"), sem("tap1"), sem("tap0")
        val_ready, gated, hidden_ready = sem("val_ready"), sem("gated"), sem("hidden_ready")
        hh_ready, hl_ready = sem("hh_ready"), sem("hl_ready")
        exponent, stored = sem("exponent"), sem("stored")
        block = es.enter_context(nc.Block())

        w_in_v = w_in[0].rearrange("(k p) n -> p k n", p=P)
        w_up_v = w_up[0].rearrange("(k p) n -> p k n", p=P)
        w_out_v = w_out[0].rearrange("(k p) n -> p k n", p=P)
        w_down_v = w_down[0].rearrange("(k p) n -> p k n", p=P)
        x_v = x[0].rearrange("(l r) d -> l r d", r=NR)
        x_blocks = x[0].rearrange("(b p) d -> p b d", p=P)
        out_v = out[0].rearrange("(l r) d -> l r d", r=NR)

        def cols(chunk):
            return chunk.rearrange("p (k n) -> p k n", k=KT)

        def rows(chunk):
            return chunk.rearrange("p (k n) -> p k n", k=2)

        def natural(t):
            return t.rearrange("p a (l r) -> p a l r", r=NR)

        def tiles(t):
            return t.rearrange("p a (r l) -> p a l r", r=NR)

        def half_slot(t, m):
            if m < DOWN_LOOP:
                return (wh if t is xTh else wl)[3][:, (m % 2) * 2 * S:(m % 2 + 1) * 2 * S].rearrange("p (k n) -> p k n", k=2)
            j = (m - DOWN_LOOP) % 4
            return t[:, 2 * j:2 * j + 2, :]

        def down_slot(m):
            return m % 2 if m < DOWN_LOOP else (2, 3, 0, 1, 2)[m - DOWN_LOOP]

        @block.sync
        def _(sp):
            def load_qkv(c, col, n):
                sp.dma_start(cols(raw[:, n % 3, :]), w_in_v[:, :, bass.ds(col, CW)]).then_inc(raw_in[n % 3], 16)

            def column(c, pair):
                g, j = CHUNKS[c]
                return (g * 3 + j) * H * E + pair * CW

            sp.dma_start(ident[:, :], ident_in).then_inc(ident_in_s, 16)
            for q in range(4):
                sp.dma_start(x_rows[:, :, q * CW:(q + 1) * CW], x_blocks[:, :, q * CW:(q + 1) * CW]).then_inc(x_in_s[q], 16)
                if q == 0:
                    load_qkv(0, column(0, 0), 0)
            load_qkv(1, column(1, 0), 1)
            sp.dma_start(const[:, :], const_in).then_inc(const_in_s, 16)
            load_qkv(2, column(2, 0), 2)
            sp.dma_start(conv_rows[0:CONV * FT, :], conv_w[0].rearrange("t (f p) -> (t f) p", p=P)).then_inc(conv_in_s, 16)
            sp.dma_start(conv_rows[CONV * FT:, :], conv_b[0].rearrange("(f p) -> f p", p=P)).then_inc(conv_in_s, 16)
            sp.wait_ge(low_ready, 1)
            load_qkv(3, column(3, 0), 3)

            def loads(pair, last):
                for c in range(1, NC + 1):
                    sp.wait_ge(low_ready, pair * NC + c + 1)
                    n = c + 3
                    if n < NC:
                        load_qkv(n, column(n, pair), n)
                    elif not last:
                        load_qkv(n - NC, column(n - NC, pair + 1), n)
                    else:
                        k = n - NC
                        sp.dma_start(rows(raw[:, n % 3, :]), w_out_v[:, 2 * k:2 * k + 2, :]).then_inc(raw_in[n % 3], 16)

            with sp.Fori(0, PAIRS - 1) as pair:
                loads(pair, False)
            loads(PAIRS - 1, True)

            sp.wait_ge(scores_ready, 4 * PAIRS)
            sp.dma_start(res[:, :, :], x_v).then_inc(res_in, 16)
            sp.wait_ge(summed, 4 * PAIRS)

            def load_ln(i):
                sp.dma_start(lnp[:, 0, :], ln_g[0, i:i + 1, :].broadcast_to([P, D])).then_inc(ln_in, 16)
                sp.dma_start(lnp[:, 1, :], ln_b[0, i:i + 1, :].broadcast_to([P, D])).then_inc(ln_in, 16)

            load_ln(0)

            def load_up(i, t):
                slot = 2 - t
                sp.dma_start(cols(raw[:, slot, :]), w_up_v[:, :, bass.ds(i * CW + t * FF, CW)]).then_inc(ff_in[t], 16)

            def load_down(m):
                t = m % 2
                sp.dma_start(rows(raw[:, 2 - t, :]), w_down_v[:, 2 * m:2 * m + 2, :]).then_inc(ff_in[t], 16)

            sp.wait_ge(low_ready, UP0 - 1)
            load_up(0, 0)
            load_up(0, 1)
            with sp.Fori(1, UP_STEPS) as i:
                sp.wait_ge(low_ready, UP0 - 1 + 2 * i)
                load_up(i, 0)
                sp.wait_ge(low_ready, UP0 + 2 * i)
                load_up(i, 1)
            for m in range(DOWN):
                sp.wait_ge(low_ready, DOWN0 + m - 1)
                load_down(m)
                if m == 0:
                    sp.wait_ge(ln_done, NR)
                    load_ln(1)
            for r in range(NR):
                sp.wait_ge(ln_done, NR + r + 1)
                sp.dma_start(out_v[:, r, :], res[:, r, :]).then_inc(stored, 16)
            sp.wait_ge(stored, 16 * NR)

        @block.tensor
        def _(pe):
            mm = nc.tensor.matmul

            def three(o, pairs):
                n = len(pairs)
                for i, ((sh, sl), (mh, ml)) in enumerate(pairs):
                    mm(o, sh, mh, start=i == 0, stop=False)
                    mm(o, sh, ml, start=False, stop=False)
                    last = mm(o, sl, mh, start=False, stop=i == n - 1)
                return last

            pe.wait_ge(ident_in_s, 16)
            for k in range(KT):
                if k % 2 == 0:
                    pe.wait_ge(x_in_s[k // 2], 16)
                for r in range(NR):
                    t = nc.tensor.transpose(bank[:, k, r * P:(r + 1) * P], x_rows[:, r, k * P:(k + 1) * P], ident[:, :])
                t.then_inc(x_turned, 1)

            def project(c, pair, free=None):
                g, j = CHUNKS[c]
                h3, l3 = cols(wh[c % 3][:, :]), cols(wl[c % 3][:, :])
                pe.wait_ge(low_ready, pair * NC + c + 1)
                if j < 2:
                    for hh in range(2):
                        t = 2 * c + hh
                        if free:
                            free(t)
                        cs = slice(hh * E, (hh + 1) * E)
                        last = three(bank[:, t % 3, :], [((h3[:, k, cs], l3[:, k, cs]), (xTh[:, k, :], xTl[:, k, :])) for k in range(KT)])
                        if hh == 0:
                            last.then_inc(qk_tile, 1)
                    last.then_inc(qk_tile, 1)
                else:
                    for i in range(NR):
                        t = QT + 4 * g + i
                        if free:
                            free(t)

                        def tok(a, k):
                            return a[:, k, i * P:(i + 1) * P] if g == 0 else a[:, k, i:S:NR]

                        last = three(bank[:, t % 3, 0:CW], [((tok(xTh, k), tok(xTl, k)), (h3[:, k, :], l3[:, k, :])) for k in range(KT)])
                        if i < NR - 1:
                            last.then_inc(v_tile, 1)
                    last.then_inc(v_tile, 1)

            def bank_free(pair):
                def free(t):
                    if t >= QT + 3:
                        pe.wait_ge(v_stored, pair * VT + t - QT - 2)
                    elif t >= 3:
                        pe.wait_ge(rope_terms, pair * QT + t - 2)
                return free

            def bank_free_next(pair):
                return lambda t: pe.wait_ge(v_stored, pair * VT + VT - 2 + t)

            def scores(source, hh):
                u = 2 * source + hh
                o = bank[:, SB + 2 * (u % 2):SB + 2 * (u % 2) + 2, :].rearrange("p a (c k) -> p (a c) k", k=CW)
                for t in range(4):
                    if source == 0:
                        lo = max(t - 1, 0) * P
                        last = mm(o[:, t, (P if t == 0 else 0):], qk[:, 0, 0, hh, t * P:(t + 1) * P],
                                  qk[:, 0, 1, hh, lo:(t + 1) * P], start=True, stop=True)
                    else:
                        for g in (1, 2):
                            ts = slice(t * P, (t + 1) * P)
                            last = mm(o[:, t, (g - 1) * P:g * P], qk[:, g % 2, 0, hh, ts], qk[:, g % 2, 1, hh, ts],
                                      start=True, stop=True)
                last.then_inc(scores_ready, 1)

            def turn(source, hh):
                u = 2 * source + hh
                o = bank[:, SB + 2 * source:SB + 2 * source + 2, :].rearrange("p a (c k) -> p (a c) k", k=P)
                for t in range(4):
                    own, other = prob[:, u, t, P:], prob[:, u, t, :P]
                    if source == 0:
                        last = nc.tensor.transpose(o[:, 2 * t, :], own, ident[:, :])
                        if t < 3:
                            last = nc.tensor.transpose(o[:, 2 * t + 1, :], prob[:, u, t + 1, :P], ident[:, :])
                    else:
                        nc.tensor.transpose(o[:, 2 * t, :], other, ident[:, :])
                        last = nc.tensor.transpose(o[:, 2 * t + 1, :], own, ident[:, :])
                last.then_inc(turned, 1)

            def weigh(source, hh):
                o = bank[:, OB, :]
                hs = slice(hh * E, (hh + 1) * E)
                pt = probT[:, source, :].rearrange("p (c k) -> p c k", k=P)
                for t in range(4):
                    if source == 0:
                        n = min(2, 4 - t)
                        last = mm(o[:, t * P:(t + n) * P], v[:, 0, t, hs], probT[:, source, 2 * t * P:(2 * t + n) * P],
                                  start=t == 0, stop=False, skip_group_check=True)
                    else:
                        for g in (1, 2):
                            last = mm(o[:, t:S:NR], v[:, g, t, hs], pt[:, 2 * t + g - 1, :],
                                      start=False, stop=t == 3 and g == 2, skip_group_check=True)
                last.then_inc(summed, 1)

            def trade():
                o = bank[:, OB, 0:P].rearrange("p (s a h r t) -> p s a h r t", s=2, a=2, h=2, r=NR)
                for s in range(2):
                    for r in range(NR):
                        last = mm(o[:, s, :, :, r, :], repT[:, s, r, :], stats[:, 0, 1 - s, :, :], start=True, stop=True)
                last.then_inc(stats_sent, 1)

            def attend(pair, last_pair):
                free = bank_free(pair)
                project(1, pair, free)
                project(2, pair, free)
                for hh in range(2):
                    pe.wait_ge(rotated, pair * QT + 3 + hh)
                    scores(0, hh)
                for c in range(3, 7):
                    project(c, pair, free)
                for hh in range(2):
                    pe.wait_ge(rotated, pair * QT + 11 + hh)
                    pe.wait_ge(masked, pair * 4 + 1 + hh)
                    scores(1, hh)
                project(7, pair, free)
                pe.wait_ge(probs_ready, pair * 4 + 4)
                trade()
                project(8, pair, free)
                if not last_pair:
                    project(0, pair + 1, bank_free_next(pair))
                pe.wait_ge(scaled, pair * 4 + 1)
                turn(0, 0)
                pe.wait_ge(scaled, pair * 4 + 2)
                turn(1, 0)
                pe.wait_ge(v_stored, pair * VT + VT)
                for n, (source, hh) in enumerate([(0, 0), (1, 0), (0, 1), (1, 1)]):
                    pe.wait_ge(turned_act, pair * 4 + n + 1)
                    pe.wait_ge(turned_dve, pair * 4 + n + 1)
                    if n == 2:
                        pe.wait_ge(head_low, pair * 2 + 1)
                    weigh(source, hh)
                    if n < 2:
                        pe.wait_ge(scaled, pair * 4 + 3 + n)
                        turn(n, 1)

            pe.wait_ge(xl_ready, KT)
            project(0, 0)
            pe.wait_ge(conv_in_s, 32)
            nc.tensor.transpose(bank[:, SB, 0:4 * FT], conv_rows[:, :], ident[0:4 * FT, 0:4 * FT]).then_inc(conv_turned, 1)
            with pe.Fori(0, PAIRS - 1) as pair:
                attend(pair, False)
            attend(PAIRS - 1, True)

            def project_out(r):
                b = SB + 2 * (r % 2)
                ts = slice(r * P, (r + 1) * P)
                if r >= 2:
                    pe.wait_ge(ln_step, LN_STEPS * (r - 2) + 1)
                for h in range(H):
                    if r == 0:
                        pe.wait_ge(low_ready, QKV_CHUNKS + h // 2 + 1)
                        if h >= H - 2:
                            pe.wait_ge(head_low, h + 1)
                    w_h, w_l = rows(wh[h // 2][:, :])[:, h % 2, :], rows(wl[h // 2][:, :])[:, h % 2, :]
                    for st, w in ((oTh, w_h), (oTh, w_l), (oTl, w_h)):
                        for half in range(2):
                            last = mm(bank[:, b + half, :], st[:, h, ts], w[:, half * S:(half + 1) * S],
                                      start=h == 0 and w is w_h and st is oTh, stop=h == H - 1 and st is oTl)
                    if r == NR - 1 and h in (1, 3):
                        last.then_inc(out_used, 1)
                last.then_inc(y_ready, 1)

            def turn_x1(r):
                b = 2 * (r % 2)
                o = bank[:, b:b + 2, :].rearrange("p a (k l) -> p (a k) l", l=P)
                pe.wait_ge(ln_done, r + 1)
                if r >= 2:
                    pe.wait_ge(x1l_ready, r - 1)
                for k in range(KT):
                    last = nc.tensor.transpose(o[:, k, :], res[:, r, k * P:(k + 1) * P], ident[:, :])
                last.then_inc(x1_turned, 1)

            for r in range(NR):
                project_out(r)
                if r >= 1:
                    turn_x1(r - 1)
            turn_x1(NR - 1)
            pe.wait_ge(x1l_ready, NR)

            with pe.Fori(0, UP_STEPS) as i:
                for t in range(2):
                    h3, l3 = cols(wh[t][:, :]), cols(wl[t][:, :])
                    pe.wait_ge(low_ready, 2 * i + UP0 + t + 1)
                    for f in range(2):
                        cs = slice(f * P, (f + 1) * P)
                        last = three(bank[:, 4 + 2 * t + f, :], [((h3[:, k, cs], l3[:, k, cs]), (xTh[:, k, :], xTl[:, k, :])) for k in range(KT)])
                        if f == 0:
                            last.then_inc(gate_ready if t == 0 else val_ready, 1)
                    last.then_inc(gate_ready if t == 0 else val_ready, 1)

            def down(m, tiles, finish):
                s = down_slot(m)
                h_h, h_l = half_slot(xTh, m), half_slot(xTl, m)
                for r in tiles:
                    ts = slice(r * P, (r + 1) * P)
                    for k in range(2):
                        for hid, w in ((h_h, wh[s]), (h_h, wl[s]), (h_l, wh[s])):
                            for half in range(2):
                                first = m == 0 and k == 0 and hid is h_h and w is wh[s]
                                last = mm(bank[:, 2 * r + half, :], hid[:, k, ts], rows(w[:, :])[:, k, half * S:(half + 1) * S],
                                          start=first, stop=finish and k == 1 and hid is h_l)
                return last

            def down_ready(m):
                pe.wait_ge(low_ready, DOWN0 + m + 1)
                pe.wait_ge(hl_ready, m + 1)

            for m in range(2):
                down_ready(m)
                if m == 0:
                    pe.wait_ge(hidden_ready, FT)
                down(m, range(NR), False).then_inc(down_used, 1)
            with pe.Fori(1, DOWN_LOOP // 2) as i:
                for t in range(2):
                    pe.wait_ge(low_ready, 2 * i + DOWN0 + t + 1)
                    pe.wait_ge(hl_ready, 2 * i + t + 1)
                    down(t + 2, range(NR), False).then_inc(down_used, 1)
            down_ready(DOWN_LOOP)
            down(DOWN_LOOP, range(NR), False).then_inc(down_used, 1)
            for r in range(NR):
                for m in range(DOWN_TAIL, DOWN):
                    if r == 0:
                        down_ready(m)
                    last = down(m, [r], m == DOWN - 1)
                last.then_inc(y_ready, 1)

        @block.scalar
        def _(sc):
            act_ = nc.scalar.activation

            def high(n_sem, count, src, dst):
                sc.wait_ge(n_sem, count)
                act_(dst[:, :], src, ACT.Copy).then_inc(high_ready, 1)

            def high_qkv(c, pair):
                high(raw_in[c % 3], pair * 48 + 16 * (c // 3 + 1), raw[:, c % 3, :], wh[c % 3])

            for k in range(KT):
                sc.wait_ge(x_turned, k + 1)
                act_(xTh[:, k, :], bank[:, k, :], ACT.Copy).then_inc(xh_ready, 1)
                if k in (3, 5):
                    high_qkv((k - 3) // 2, 0)
            high_qkv(2, 0)
            sc.wait_ge(conv_turned, 1)
            act_(convp[:, :], bank[:, SB, 0:4 * FT], ACT.Copy).then_inc(conv_ready, 1)

            def next_high(c, pair):
                g, j = CHUNKS[c % NC]
                if j < 2:
                    sc.wait_ge(qk_tile, (pair + c // NC) * QT + 2 * (c % NC) + 2)
                else:
                    sc.wait_ge(v_tile, pair * VT + 4 * (g + 1))
                high_qkv(c + 3, pair)

            def exps(u, pair):
                sc.wait_ge(shift_ready, pair * 4 + u + 1)
                for t in range(4):
                    lo = P if u < 2 and t == 0 else 0
                    c = 4 * (u % 2) + t
                    last = act_(prob[:, u, t, lo:], prob[:, u, t, lo:], ACT.Exp, bias=stats[:, 0, u // 2, 0, c:c + 1],
                                accum_out=stats[:, 0, u // 2, 1, c:c + 1])
                last.then_inc(probs_ready, 1)

            def store_v(g, tiles, pair):
                for i in tiles:
                    t = 4 * g + i
                    sc.wait_ge(v_tile, pair * VT + t + 1)
                    act_(v[:, g, i, :], bank[:, (QT + t) % 3, 0:CW], ACT.Copy).then_inc(v_stored, 1)

            next_high(0, 0)

            def attend(pair, last_pair):
                next_high(1, pair)
                next_high(2, pair)
                exps(0, pair)
                exps(1, pair)
                for c in range(3, 6):
                    next_high(c, pair)
                store_v(0, range(4), pair)
                next_high(6, pair)
                store_v(1, (0,), pair)
                exps(2, pair)
                store_v(1, (1, 2), pair)
                exps(3, pair)
                store_v(1, (3,), pair)
                next_high(7, pair)
                store_v(2, (0,), pair)
                sc.wait_ge(merge_step, pair * 7 + 4)
                act_(mweight[:, :, :, :], merge[:, 1:3, :, :], ACT.Exp).then_inc(mweight_ready, 1)
                store_v(2, (1, 2, 3), pair)
                next_high(8, pair)
                if not last_pair:
                    next_high(9, pair)
                for n, (source, hh) in enumerate([(0, 0), (1, 0), (0, 1), (1, 1)]):
                    if n == 3:
                        head(0, pair)
                    sc.wait_ge(turned, pair * 4 + n + 1)
                    if n >= 2:
                        sc.wait_ge(summed, pair * 4 + n - 1)
                    act_(probT[:, source, 0:S], bank[:, SB + 2 * source, :], ACT.Copy).then_inc(turned_act, 1)
                head(1, pair)

            def head(hh, pair):
                sc.wait_ge(summed, pair * 4 + 2 * hh + 2)
                act_(tiles(oTh[:, bass.ds(2 * pair + hh, 1), :]), natural(bank[:, OB:OB + 1, :]), ACT.Copy).then_inc(head_high, 1)

            with sc.Fori(0, PAIRS - 1) as pair:
                attend(pair, False)
            attend(PAIRS - 1, True)
            high(raw_in[0], 16 * (QKV_CHUNKS // 3 + 1 + 0) + 16, raw[:, 0, :], wh[3])

            def normalise(i, r):
                sc.wait_ge(ln_step, LN_STEPS * (NR * i + r + 1))
                act_(res[:, r, :], zrow[:, :], ACT.Identity, scale=small[:, 14:15], bias=small[:, 15:16]).then_inc(normed, 1)

            for r in range(NR):
                normalise(0, r)
                sc.wait_ge(x1_turned, r + 1)
                b = 2 * (r % 2)
                act_(xTh[:, :, :].rearrange("p k (l r) -> p k l r", r=NR)[:, :, :, r],
                     bank[:, b:b + 2, :].rearrange("p a (k l) -> p (a k) l", l=P), ACT.Copy).then_inc(x1h_ready, 1)
                if r == NR - 2:
                    for t in range(2):
                        sc.wait_ge(out_used, t + 1)
                        high(ff_in[t], 16, raw[:, 2 - t, :], wh[t])

            def hidden_high(m, count=None):
                sc.wait_ge(hidden_ready, 2 * m + 2)
                act_(half_slot(xTh, m), hidden[:, 2 * m:2 * m + 2, :], ACT.Copy).then_inc(hh_ready, 1)

            with sc.Fori(0, UP_STEPS) as i:
                for f in range(2):
                    sc.wait_ge(gate_ready, 2 * i + f + 1)
                    act_(cv[:, f, :], bank[:, 4 + f, :], ACT.Identity, scale=convp[:, bass.ds(2 * i + (2 * FT + f), 1)],
                         bias=convp[:, bass.ds(2 * i + (3 * FT + f), 1)]).then_inc(tap2, 1)
                sc.wait_ge(gate_ready, 2 * i + 2)
                high(ff_in[0], 16 * i + 32, raw[:, 2, :], wh[0])
                for f in range(2):
                    sc.wait_ge(tap0, 2 * i + f + 1)
                    act_(act[:, f, :], cv[:, f, :], ACT.Silu).then_inc(gated, 1)
                sc.wait_ge(gated, 2 * i + 2)
                sc.wait_ge(val_ready, 2 * i + 2)
                high(ff_in[1], 16 * i + 32, raw[:, 1, :], wh[1])
            hidden_high(0)
            hidden_high(1)
            for m in range(2, DOWN):
                used = {DOWN_LOOP: None, 7: 5, 8: 4, 9: 5, 10: 6}.get(m, m - 2)
                if used is not None:
                    sc.wait_ge(down_used, used + 1)
                high(ff_in[m % 2], 16 * (UP_STEPS + m // 2 + 1), raw[:, 2 - m % 2, :], wh[down_slot(m)])
                hidden_high(m)
            for r in range(NR):
                normalise(1, r)

        @block.vector
        def _(dv):
            tt, ts_, stt = nc.vector.tensor_tensor, nc.vector.tensor_scalar, nc.vector.scalar_tensor_tensor

            def low(count, src, hi, dst):
                dv.wait_ge(high_ready, count)
                tt(dst[:, :], src, hi[:, :].bitcast(F32), ALU.subtract).then_inc(low_ready, 1)

            def low_qkv(c, pair):
                low(pair * NC + c + 1, raw[:, c % 3, :], wh[c % 3], wl[c % 3])

            for k in range(KT):
                dv.wait_ge(xh_ready, k + 1)
                tt(xTl[:, k, :], bank[:, k, :], xTh[:, k, :].bitcast(F32), ALU.subtract).then_inc(xl_ready, 1)
                if k in (4, 6):
                    low_qkv((k - 4) // 2, 0)
            low_qkv(2, 0)
            dv.wait_ge(const_in_s, 16)
            dv.wait_ge(conv_ready, 1)

            def rope(c, pair):
                g, j = CHUNKS[c]
                for hh in range(2):
                    t = 2 * c + hh
                    b = bank[:, t % 3, :]
                    dv.wait_ge(qk_tile, pair * QT + t + 1)
                    if t >= 2:
                        dv.wait_ge(rotated, pair * QT + t - 1)
                    by_cos, bc, cc = qk[:, g % 2, j, hh:hh + 1, :], bank[:, t % 3:t % 3 + 1, :], cosT.rearrange("p (o n) -> p o n", o=1)
                    if g > 0:
                        by_cos, bc, cc = tiles(by_cos), natural(bc), natural(cc)
                    tt(by_cos, bc, cc, ALU.mult)
                    tt(swapped[64:128, hh, :], b[0:64, :], sinT[0:64, :], ALU.mult)
                    tt(swapped[0:64, hh, :], b[64:128, :], sinT[64:128, :], ALU.mult).then_inc(rope_terms, 1)

            def mask(source, pair):
                for hh in range(2):
                    u = 2 * source + hh
                    dv.wait_ge(scores_ready, pair * 4 + u + 1)
                    ps = bank[:, SB + 2 * hh:SB + 2 * hh + 2, :].rearrange("p a (c k) -> p (a c) k", k=CW)
                    m = maskT[:, source:source + 1, :]
                    t0 = 1 - source
                    if source == 0:
                        stt(prob[:, u, 0, P:], ps[:, 0, P:], SCALE, maskT[:, 0, P:], ALU.mult, ALU.add)
                    stt(prob[:, u, t0:, :], ps[:, t0:, :], SCALE, m.broadcast_to([P, 4 - t0, CW]), ALU.mult, ALU.add).then_inc(masked, 1)
                for hh in range(2):
                    u = 2 * source + hh
                    c = 4 * hh
                    t0 = 1 - source
                    dv.wait_ge(masked, pair * 4 + u + 1)
                    if source == 0:
                        nc.vector.tensor_reduce(stats[:, 0, source, 0, c:c + 1], prob[:, u, 0, P:], X, ALU.max, negate=True)
                    nc.vector.tensor_reduce(stats[:, 0, source, 0, c + t0:c + 4], prob[:, u, t0:, :], X, ALU.max, negate=True).then_inc(shift_ready, 1)

            def merge_sources(pair):
                step = [0]

                def link(ins):
                    step[0] += 1
                    ins.then_inc(merge_step, 1)
                    dv.wait_ge(merge_step, pair * 7 + step[0])

                dv.wait_ge(stats_sent, pair + 1)
                ex = bank[:, OB, 0:P].rearrange("p (s x t) -> p s x t", s=2, t=NR)
                link(tt(picked[:, :, :].rearrange("p (s x) t -> p s x t", s=2), ex, selT.broadcast_to([P, 2, 16, NR]), ALU.mult))
                link(nc.vector.tensor_reduce(stats[:, 1, :, :, :].rearrange("p s a c -> p (s a c)"), picked[:, :, :], X, ALU.add))
                link(tt(merge[:, 0, :, :], stats[:, 0, :, 0, :], stats[:, 1, :, 0, :], ALU.min))
                link(tt(merge[:, 1:3, :, :], merge[:, 0:1, :, :].broadcast_to([P, 2, 2, 8]), stats[:, :, :, 0, :], ALU.subtract))
                dv.wait_ge(mweight_ready, pair + 1)
                link(tt(merge[:, 3:5, :, :], mweight[:, :, :, :], stats[:, :, :, 1, :], ALU.mult))
                link(tt(merge[:, 0, :, :], merge[:, 3, :, :], merge[:, 4, :, :], ALU.add))
                link(nc.vector.reciprocal(merge[:, 3, :, :], merge[:, 0, :, :]))
                tt(coef[:, :, :], mweight[:, 0, :, :], merge[:, 3, :, :], ALU.mult).then_inc(coef_ready, 1)

            def scale(pair):
                dv.wait_ge(coef_ready, pair + 1)
                for source, hh in ((0, 0), (1, 0), (0, 1), (1, 1)):
                    u = 2 * source + hh
                    for t in range(4):
                        lo = P if source == 0 and t == 0 else 0
                        c = 4 * hh + t
                        last = ts_(prob[:, u, t, lo:], prob[:, u, t, lo:], coef[:, source, c:c + 1], None, ALU.mult)
                    last.then_inc(scaled, 1)

            rope(0, 0)
            low_qkv(3, 0)

            def attend(pair, last_pair):
                rope(1, pair)
                low_qkv(4, pair)
                rope(2, pair)
                low_qkv(5, pair)
                mask(0, pair)
                for c in range(3, 6):
                    rope(c, pair)
                    low_qkv(c + 3, pair)
                low_qkv(9, pair)
                mask(1, pair)
                low_qkv(10, pair)
                merge_sources(pair)
                scale(pair)
                low_qkv(11, pair)
                if not last_pair:
                    rope(0, pair + 1)
                    low_qkv(12, pair)
                for n, (source, hh) in enumerate([(0, 0), (1, 0), (0, 1), (1, 1)]):
                    if n == 3:
                        head(0, pair)
                    dv.wait_ge(turned, pair * 4 + n + 1)
                    if n >= 2:
                        dv.wait_ge(summed, pair * 4 + n - 1)
                    w = S if source else 3 * P
                    nc.vector.tensor_copy(probT[:, source, S:S + w], bank[:, SB + 2 * source + 1, 0:w]).then_inc(turned_dve, 1)
                head(1, pair)

            def head(hh, pair):
                dv.wait_ge(head_high, pair * 2 + hh + 1)
                h = bass.ds(2 * pair + hh, 1)
                tt(tiles(oTl[:, h, :]), natural(bank[:, OB:OB + 1, :]), tiles(oTh[:, h, :]).bitcast(F32), ALU.subtract).then_inc(head_low, 1)

            with dv.Fori(0, PAIRS - 1) as pair:
                attend(pair, False)
            attend(PAIRS - 1, True)
            low(UP0, raw[:, 0, :], wh[3], wl[3])

            def statistics(i, r):
                n = LN_STEPS * (NR * i + r)
                ps = bank[:, SB + 2 * (r % 2):SB + 2 * (r % 2) + 2, :] if i == 0 else bank[:, 2 * r:2 * r + 2, :]
                dv.wait_ge(y_ready, NR * i + r + 1)
                if NR * i + r >= 1:
                    dv.wait_ge(normed, NR * i + r)
                stt(zrow[:, :], res[:, r, :], ALPHA, ps.rearrange("p a n -> p (a n)"), ALU.mult, ALU.add).then_inc(ln_step, 1)
                dv.wait_ge(ln_step, n + 1)
                nc.vector.bn_stats(small[:, 0:6], zrow[:, 0:S])
                nc.vector.bn_stats(small[:, 6:12], zrow[:, S:]).then_inc(ln_step, 1)
                dv.wait_ge(ln_step, n + 2)
                nc.vector.bn_aggr(small[:, 12:14], small[:, 0:12]).then_inc(ln_step, 1)
                dv.wait_ge(ln_step, n + 3)
                nc.vector.tensor_scalar_add(small[:, 13:14], small[:, 13:14], EPS).then_inc(ln_step, 1)
                dv.wait_ge(ln_step, n + 5)
                stt(small[:, 15:16], small[:, 12:13], -1.0, small[:, 14:15], ALU.mult, ALU.mult).then_inc(ln_step, 1)

            def gain(i, r):
                dv.wait_ge(normed, NR * i + r + 1)
                if r == 0:
                    dv.wait_ge(ln_in, 32 * i + 32)
                tt(res[:, r, :], res[:, r, :], lnp[:, 0, :], ALU.mult).then_inc(scaled_g, 1)

            def x1_low(r):
                b = 2 * (r % 2)
                view = (lambda t: t[:, :, :].rearrange("p k (l r) -> p k l r", r=NR)[:, :, :, r])
                dv.wait_ge(x1h_ready, r + 1)
                tt(view(xTl), bank[:, b:b + 2, :].rearrange("p a (k l) -> p (a k) l", l=P), view(xTh).bitcast(F32), ALU.subtract).then_inc(x1l_ready, 1)

            dv.wait_ge(res_in, 16)
            for r in range(NR):
                statistics(0, r)
                gain(0, r)
                if r >= 1:
                    x1_low(r - 1)
            x1_low(NR - 1)

            for t in range(2):
                low(UP0 + t + 1, raw[:, 2 - t, :], wh[t], wl[t])

            with dv.Fori(0, UP_STEPS) as i:
                for f in range(2):
                    dv.wait_ge(tap2, 2 * i + f + 1)
                    stt(cv[:, f, 1:], bank[:, 4 + f, 0:S - 1], convp[:, bass.ds(2 * i + (FT + f), 1)], cv[:, f, 1:], ALU.mult, ALU.add).then_inc(tap1, 1)
                for f in range(2):
                    dv.wait_ge(tap1, 2 * i + f + 1)
                    stt(cv[:, f, 2:], bank[:, 4 + f, 0:S - 2], convp[:, bass.ds(2 * i + f, 1)], cv[:, f, 2:], ALU.mult, ALU.add).then_inc(tap0, 1)
                low(2 * i + UP0 + 3, raw[:, 2, :], wh[0], wl[0])
                for f in range(2):
                    dv.wait_ge(gated, 2 * i + f + 1)
                    dv.wait_ge(val_ready, 2 * i + f + 1)
                    tt(tiles(hidden[:, bass.ds(2 * i + f, 1), :]), natural(act[:, f:f + 1, :]), natural(bank[:, 6 + f:7 + f, :]),
                       ALU.mult).then_inc(hidden_ready, 1)
                low(2 * i + UP0 + 4, raw[:, 1, :], wh[1], wl[1])

            def hidden_low(m):
                dv.wait_ge(hh_ready, m + 1)
                tt(half_slot(xTl, m), hidden[:, 2 * m:2 * m + 2, :], half_slot(xTh, m).bitcast(F32), ALU.subtract).then_inc(hl_ready, 1)

            hidden_low(0)
            hidden_low(1)
            for m in range(2, DOWN):
                s = down_slot(m)
                low(DOWN0 + m + 1, raw[:, 2 - m % 2, :], wh[s], wl[s])
                hidden_low(m)
            for r in range(NR):
                statistics(1, r)
                gain(1, r)

        @block.gpsimd
        def _(pool):
            def add_terms(c, pair):
                g, j = CHUNKS[c]
                for hh in range(2):
                    pool.wait_ge(rope_terms, pair * QT + 2 * c + hh + 1)
                    a, b = qk[:, g % 2, j, hh:hh + 1, :], swapped[:, hh:hh + 1, :]
                    if g > 0:
                        a, b = tiles(a), natural(b)
                    nc.gpsimd.tensor_tensor(a, a, b, ALU.add).then_inc(rotated, 1)

            nc.gpsimd.memset(small[:, 16:17], -0.5).then_inc(exponent, 1)
            add_terms(0, 0)

            def attend(pair, last_pair):
                for c in range(1, 6):
                    add_terms(c, pair)
                if not last_pair:
                    add_terms(0, pair + 1)

            with pool.Fori(0, PAIRS - 1) as pair:
                attend(pair, False)
            attend(PAIRS - 1, True)

            pool.wait_ge(exponent, 1)
            for i in range(2):
                for r in range(NR):
                    pool.wait_ge(ln_step, LN_STEPS * (NR * i + r) + 4)
                    nc.gpsimd.tensor_tensor(small[:, 14:15], small[:, 13:14], small[:, 16:17], ALU.pow).then_inc(ln_step, 1)
                    pool.wait_ge(scaled_g, NR * i + r + 1)
                    nc.gpsimd.tensor_tensor(res[:, r, :], res[:, r, :], lnp[:, 1, :], ALU.add).then_inc(ln_done, 1)


def kernel(x, attn_w_in, attn_w_out, ffn_w_up, ffn_conv_w, ffn_conv_b, ffn_w_down, ln_g, ln_b, **unused):
    import concourse.bacc as bacc
    from concourse.bass_utils import run_bass_kernel_spmd

    nc = bacc.Bacc("TRN2", target_bir_lowering=False, num_devices=1)
    arrays = {
        "x": x, "w_in": attn_w_in, "w_out": attn_w_out, "w_up": ffn_w_up, "conv_w": ffn_conv_w,
        "conv_b": ffn_conv_b, "w_down": ffn_w_down, "ln_g": ln_g, "ln_b": ln_b,
        "ident": np.eye(P, dtype=np.float32), "const": constants(),
    }
    arrays = {n: np.ascontiguousarray(a) for n, a in arrays.items()}
    args = [nc.dram_tensor(f"in_{n}", a.shape, F32, kind="ExternalInput").ap() for n, a in arrays.items()]
    out = nc.dram_tensor("out", (1, S, D), F32, kind="ExternalOutput").ap()
    layer(nc, *args, out)
    r = run_bass_kernel_spmd(nc, [{f"in_{n}": a for n, a in arrays.items()}], core_ids=[0])
    return r.results[0]["out"]
```

```python
import math
from contextlib import ExitStack

import numpy as np

import concourse.bass as bass
from concourse import mybir

F32 = mybir.dt.float32
F32R = mybir.dt.float32r
ALU = mybir.AluOpType
ACT = mybir.ActivationFunctionType
X = mybir.AxisListType.X

P = 128
S = 512
D = 1024
KT = D // P
NR = 4
G = 3
H = 8
E = 128
PAIRS = H // 2
FF = 2816
FT = FF // P
CONV = 3
CW = 256
ALPHA = 2.0 ** 0.25
EPS = 1e-5
Y_BANK = (0, 4, 6, 4)
T_BANK = (2, 0, 2, 0)
GATE_BANK, VAL_BANK = 6, 4
EARLY = 3 * P
SCALE = E ** -0.5
NEG = -1e30

CHUNKS = [(g, j) for g in range(G) for j in (0, 1)] + [(g, 2) for g in range(G)]
NC = len(CHUNKS)
QT = 12
VT = 12
OUT_CHUNKS = 4
QKV_CHUNKS = PAIRS * NC
UP0 = QKV_CHUNKS + OUT_CHUNKS
UP_STEPS = FT // 2
DOWN0 = UP0 + 2 * UP_STEPS
DOWN = FT // 2
DOWN_LOOP = 6
DOWN_TAIL = 7

C_COS, C_SIN, C_MASK, C_REP, C_SEL = 0, S, 2 * S, 2 * S + 512, 2 * S + 1536
C_ALL = C_SEL + 2 * NR


def constants():
    pos = np.arange(S, dtype=np.float32)
    inv = (np.float32(10000.0) ** (-np.arange(0, E, 2, dtype=np.float32) / np.float32(E))).astype(np.float32)
    ang = (inv[:, None] * pos[None, :]).astype(np.float32)
    out = np.zeros((P, C_ALL), np.float32)
    out[:64, C_COS:C_COS + S] = out[64:, C_COS:C_COS + S] = np.cos(ang.astype(np.float64))
    sin = np.sin(ang.astype(np.float64))
    out[:64, C_SIN:C_SIN + S], out[64:, C_SIN:C_SIN + S] = sin, -sin
    q, k = np.arange(P)[:, None], np.arange(P)[None, :]
    mask = np.full((P, 2, CW), NEG, np.float32)
    mask[:, 0, :P][k >= q] = 0
    mask[:, 0, P:][k <= q] = 0
    mask[:, 1, :P][k <= q] = 0
    mask[:, 1, P:][(k <= q) & ((q - k) % 4 == 0)] = 0
    out[:, C_MASK:C_MASK + 512] = mask.reshape(P, 512)
    rep, sel = np.zeros((P, 2, NR, P), np.float32), np.zeros((P, 2, NR), np.float32)
    p = np.arange(P)
    for t in range(NR):
        rep[32 * t + p // 4, 0, t, p] = 1
        rep[4 * (p % 32) + t, 1, t, p] = 1
    sel[p, 0, p % 4] = 1
    sel[p, 1, p // 32] = 1
    out[:, C_REP:C_REP + 1024] = rep.reshape(P, 1024)
    out[:, C_SEL:C_SEL + 8] = sel.reshape(P, 8)
    return out


def layer(nc, x, w_in, w_out, w_up, conv_w, conv_b, w_down, ln_g, ln_b, ident_in, const_in, out):
    es = ExitStack()
    with es:
        def sb(name, shape, dt=F32, scope=es):
            return scope.enter_context(nc.sbuf_tensor(name, shape, dt))

        def sem(name):
            return es.enter_context(nc.semaphore(name))

        raw = sb("raw", [P, 3, KT * CW])
        wh = [sb(f"wh{s}", [P, KT * CW], F32R) for s in range(3)]
        wl = [sb(f"wl{s}", [P, KT * CW], F32R) for s in range(3)]
        xTh = sb("xTh", [P, KT, S], F32R)
        xTl = sb("xTl", [P, KT, S], F32R)
        ident = sb("ident", [P, P])
        convp = sb("convp", [P, 4 * FT])
        small = sb("small", [P, 64])
        with ExitStack() as s0:
            x_rows = sb("x_rows", [P, NR, D], scope=s0)
            conv_rows = sb("conv_rows", [4 * FT, P], scope=s0)
        with ExitStack() as s1:
            qk = sb("qk", [P, 2, 2, 2, S], scope=s1)
            v = sb("v", [P, G, NR, CW], scope=s1)
            prob = sb("prob", [P, 4, NR, CW], scope=s1)
            probT = sb("probT", [P, 2, 8 * P], scope=s1)
            swapped = sb("swapped", [P, 2, S], scope=s1)
            oTh = sb("oTh", [P, H, S], F32R, scope=s1)
            oTl = sb("oTl", [P, H, S], F32R, scope=s1)
            const = sb("const", [P, C_ALL], scope=s1)
            stats = sb("stats", [P, 2, 2, 2, 8], scope=s1)
            picked = sb("picked", [P, 32, NR], scope=s1)
            merge = sb("merge", [P, 5, 2, 8], scope=s1)
            coef = sb("coef", [P, 2, 8], scope=s1)
            mweight = sb("mweight", [P, 2, 2, 8], scope=s1)
        with ExitStack() as s2:
            res = sb("res", [P, NR, D], scope=s2)
            lnp = sb("lnp", [P, 2, D], scope=s2)
            zrow = sb("zrow", [P, D], scope=s2)
            wh.append(sb("wh3", [P, KT * CW], F32R, scope=s2))
            wl.append(sb("wl3", [P, KT * CW], F32R, scope=s2))
            hidden = sb("hidden", [P, FT, S], scope=s2)
            cv = sb("cv", [P, 2, S], scope=s2)
            act = sb("act", [P, 2, S], scope=s2)
        bank = es.enter_context(nc.psum_tensor("bank", [P, 8, S], F32))
        OB, SB = 3, 4

        cosT, sinT = const[:, C_COS:C_COS + S], const[:, C_SIN:C_SIN + S]
        maskT = const[:, C_MASK:C_MASK + 512].rearrange("p (s k) -> p s k", s=2)
        repT = const[:, C_REP:C_REP + 1024].rearrange("p (s r k) -> p s r k", s=2, r=NR)
        selT = const[:, C_SEL:C_SEL + 8].rearrange("p (s o t) -> p s o t", s=2, o=1)

        ident_in_s, const_in_s, conv_in_s = sem("ident_loaded"), sem("const_loaded"), sem("conv_loaded")
        x_in_s = [sem(f"x_loaded{q}") for q in range(4)]
        raw_in = [sem(f"raw_loaded{s}") for s in range(3)]
        ff_in = [sem(f"ff_loaded{s}") for s in range(2)]
        high_ready, low_ready = sem("high_ready"), sem("low_ready")
        out_used, down_used = sem("out_used"), sem("down_used")
        x_turned, xh_ready, xl_ready = sem("x_turned"), sem("xh_ready"), sem("xl_ready")
        conv_turned, conv_ready = sem("conv_turned"), sem("conv_ready")
        qk_tile, v_tile = sem("qk_tile"), sem("v_tile")
        rope_terms, rotated = sem("rope_terms"), sem("rotated")
        v_stored = sem("v_stored")
        scores_ready, masked, shift_ready = sem("scores_ready"), sem("masked"), sem("shift_ready")
        probs_ready, stats_sent, merge_step = sem("probs_ready"), sem("stats_sent"), sem("merge_step")
        mweight_ready, coef_ready, scaled = sem("mweight_ready"), sem("coef_ready"), sem("scaled")
        turned, turned_act, turned_dve = sem("turned"), sem("turned_act"), sem("turned_dve")
        summed, head_high, head_low = sem("summed"), sem("head_high"), sem("head_low")
        res_in, ln_in = sem("res_loaded"), sem("ln_loaded")
        y_ready, y_half = sem("y_ready"), sem("y_half")
        z_ready, ln_stats, rstd_ready, centred, ln_done = sem("z_ready"), sem("ln_stats"), sem("rstd_ready"), sem("centred"), sem("ln_done")
        first_in, first_high, first_low = sem("first_loaded"), sem("first_high"), sem("first_low")
        x1_turned, x1h_ready, x1l_ready = sem("x1_turned"), sem("x1h_ready"), sem("x1l_ready")
        gate_ready, tap2, tap1, tap0 = sem("gate_ready"), sem("tap2"), sem("tap1"), sem("tap0")
        val_ready, gated, hidden_ready = sem("val_ready"), sem("gated"), sem("hidden_ready")
        hh_ready, hl_ready = sem("hh_ready"), sem("hl_ready")
        exponent, stored = sem("exponent"), sem("stored")
        block = es.enter_context(nc.Block())

        w_in_v = w_in[0].rearrange("(k p) n -> p k n", p=P)
        w_up_v = w_up[0].rearrange("(k p) n -> p k n", p=P)
        w_out_v = w_out[0].rearrange("(k p) n -> p k n", p=P)
        w_down_v = w_down[0].rearrange("(k p) n -> p k n", p=P)
        x_blocks = x[0].rearrange("(b p) d -> p b d", p=P)
        out_blocks = out[0].rearrange("(b p) d -> p b d", p=P)

        def cols(chunk):
            return chunk.rearrange("p (k n) -> p k n", k=KT)

        def rows(chunk):
            return chunk.rearrange("p (k n) -> p k n", k=2)

        def natural(t):
            return t.rearrange("p a (l r) -> p a l r", r=NR)

        def tiles(t):
            return t.rearrange("p a (r l) -> p a l r", r=NR)

        def half_slot(t, m):
            if m < DOWN_LOOP:
                return (wh if t is xTh else wl)[3][:, (m % 2) * 2 * S:(m % 2 + 1) * 2 * S].rearrange("p (k n) -> p k n", k=2)
            j = (m - DOWN_LOOP) % 4
            return t[:, 2 * j:2 * j + 2, :]

        def down_slot(m):
            return m % 2 if m < DOWN_LOOP else (2, 3, 0, 1, 2)[m - DOWN_LOOP]

        @block.sync
        def _(sp):
            def load_qkv(c, col, n):
                sp.dma_start(cols(raw[:, n % 3, :]), w_in_v[:, :, bass.ds(col, CW)]).then_inc(raw_in[n % 3], 16)

            def column(c, pair):
                g, j = CHUNKS[c]
                return (g * 3 + j) * H * E + pair * CW

            sp.dma_start(ident[:, :], ident_in).then_inc(ident_in_s, 16)
            half, c0 = KT // 2, column(0, 0)
            sp.dma_start(cols(raw[:, 0, :])[:, :half, :], w_in_v[:, :half, c0:c0 + CW]).then_inc(first_in, 16)
            sp.dma_start(x_rows[:, :, 0:CW], x_blocks[:, :, 0:CW]).then_inc(x_in_s[0], 16)
            sp.dma_start(cols(raw[:, 0, :])[:, half:, :], w_in_v[:, half:, c0:c0 + CW]).then_inc(raw_in[0], 16)
            for q in range(1, 4):
                sp.dma_start(x_rows[:, :, q * CW:(q + 1) * CW], x_blocks[:, :, q * CW:(q + 1) * CW]).then_inc(x_in_s[q], 16)
            load_qkv(1, column(1, 0), 1)
            sp.dma_start(const[:, :], const_in).then_inc(const_in_s, 16)
            load_qkv(2, column(2, 0), 2)
            sp.dma_start(conv_rows[0:CONV * FT, :], conv_w[0].rearrange("t (f p) -> (t f) p", p=P)).then_inc(conv_in_s, 16)
            sp.dma_start(conv_rows[CONV * FT:, :], conv_b[0].rearrange("(f p) -> f p", p=P)).then_inc(conv_in_s, 16)
            sp.wait_ge(low_ready, 1)
            load_qkv(3, column(3, 0), 3)

            def loads(pair, last):
                for c in range(1, NC + 1):
                    sp.wait_ge(low_ready, pair * NC + c + 1)
                    n = c + 3
                    if n < NC:
                        load_qkv(n, column(n, pair), n)
                    elif not last:
                        load_qkv(n - NC, column(n - NC, pair + 1), n)
                    else:
                        k = n - NC
                        sp.dma_start(rows(raw[:, n % 3, :]), w_out_v[:, 2 * k:2 * k + 2, :]).then_inc(raw_in[n % 3], 16)

            with sp.Fori(0, PAIRS - 1) as pair:
                loads(pair, False)
            loads(PAIRS - 1, True)

            sp.wait_ge(scores_ready, 4 * PAIRS)
            sp.dma_start(res[:, :, :], x_blocks).then_inc(res_in, 16)
            sp.wait_ge(summed, 4 * PAIRS)

            def load_ln(i):
                sp.dma_start(lnp[:, 0, :], ln_g[0, i:i + 1, :].broadcast_to([P, D])).then_inc(ln_in, 16)
                sp.dma_start(lnp[:, 1, :], ln_b[0, i:i + 1, :].broadcast_to([P, D])).then_inc(ln_in, 16)

            load_ln(0)

            def load_up(i, t):
                slot = 2 - t
                sp.dma_start(cols(raw[:, slot, :]), w_up_v[:, :, bass.ds(i * CW + t * FF, CW)]).then_inc(ff_in[t], 16)

            def load_down(m):
                t = m % 2
                sp.dma_start(rows(raw[:, 2 - t, :]), w_down_v[:, 2 * m:2 * m + 2, :]).then_inc(ff_in[t], 16)

            sp.wait_ge(low_ready, UP0 - 1)
            load_up(0, 0)
            load_up(0, 1)
            with sp.Fori(1, UP_STEPS) as i:
                sp.wait_ge(low_ready, UP0 - 1 + 2 * i)
                load_up(i, 0)
                sp.wait_ge(low_ready, UP0 + 2 * i)
                load_up(i, 1)
            for m in range(DOWN):
                sp.wait_ge(low_ready, DOWN0 + m - 1)
                load_down(m)
                if m == 0:
                    sp.wait_ge(ln_done, 2 * NR)
                    load_ln(1)
            for r in range(NR - 1):
                sp.wait_ge(ln_done, 2 * (NR + r + 1))
                sp.dma_start(out_blocks[:, r, :], res[:, r, :]).then_inc(stored, 16)
            for half in range(2):
                sp.wait_ge(ln_done, 4 * NR - 1 + half)
                hs = slice(half * S, (half + 1) * S)
                sp.dma_start(out_blocks[:, NR - 1, hs], res[:, NR - 1, hs]).then_inc(stored, 16)
            sp.wait_ge(stored, 16 * (NR + 1))

        @block.tensor
        def _(pe):
            mm = nc.tensor.matmul

            def three(o, pairs, before=None):
                n = len(pairs)
                for i, ((sh, sl), (mh, ml)) in enumerate(pairs):
                    if before:
                        before(i)
                    mm(o, sh, mh, start=i == 0, stop=False)
                    mm(o, sh, ml, start=False, stop=False)
                    last = mm(o, sl, mh, start=False, stop=i == n - 1)
                return last

            pe.wait_ge(ident_in_s, 16)
            for k in range(KT):
                if k % 2 == 0:
                    pe.wait_ge(x_in_s[k // 2], 16)
                for r in range(NR):
                    t = nc.tensor.transpose(bank[:, k, r * P:(r + 1) * P], x_rows[:, r, k * P:(k + 1) * P], ident[:, :])
                t.then_inc(x_turned, 1)

            def project(c, pair, free=None, before=None, between=None):
                g, j = CHUNKS[c]
                h3, l3 = cols(wh[c % 3][:, :]), cols(wl[c % 3][:, :])
                if not before:
                    pe.wait_ge(low_ready, pair * NC + c + 1)
                if j < 2:
                    for hh in range(2):
                        t = 2 * c + hh
                        if free:
                            free(t)
                        cs = slice(hh * E, (hh + 1) * E)
                        last = three(bank[:, t % 3, :], [((h3[:, k, cs], l3[:, k, cs]), (xTh[:, k, :], xTl[:, k, :])) for k in range(KT)],
                                     before if hh == 0 else None)
                        if hh == 0:
                            last.then_inc(qk_tile, 1)
                            if between:
                                between()
                    last.then_inc(qk_tile, 1)
                else:
                    for i in range(NR):
                        t = QT + 4 * g + i
                        if free:
                            free(t)

                        def tok(a, k):
                            return a[:, k, i * P:(i + 1) * P] if g == 0 else a[:, k, i:S:NR]

                        last = three(bank[:, t % 3, 0:CW], [((tok(xTh, k), tok(xTl, k)), (h3[:, k, :], l3[:, k, :])) for k in range(KT)])
                        if i < NR - 1:
                            last.then_inc(v_tile, 1)
                    last.then_inc(v_tile, 1)

            def bank_free(pair):
                def free(t):
                    if t >= QT + 3:
                        pe.wait_ge(v_stored, pair * VT + t - QT - 2)
                    elif t >= 3:
                        pe.wait_ge(rope_terms, pair * QT + t - 2)
                return free

            def bank_free_next(pair):
                return lambda t: pe.wait_ge(v_stored, pair * VT + VT - 2 + t)

            def scores(source, hh):
                u = 2 * source + hh
                o = bank[:, SB + 2 * (u % 2):SB + 2 * (u % 2) + 2, :].rearrange("p a (c k) -> p (a c) k", k=CW)
                for t in range(4):
                    if source == 0:
                        lo = max(t - 1, 0) * P
                        last = mm(o[:, t, (P if t == 0 else 0):], qk[:, 0, 0, hh, t * P:(t + 1) * P],
                                  qk[:, 0, 1, hh, lo:(t + 1) * P], start=True, stop=True)
                    else:
                        for g in (1, 2):
                            ts = slice(t * P, (t + 1) * P)
                            last = mm(o[:, t, (g - 1) * P:g * P], qk[:, g % 2, 0, hh, ts], qk[:, g % 2, 1, hh, ts],
                                      start=True, stop=True)
                last.then_inc(scores_ready, 1)

            def turn(source, hh):
                u = 2 * source + hh
                o = bank[:, SB + 2 * source:SB + 2 * source + 2, :].rearrange("p a (c k) -> p (a c) k", k=P)
                for t in range(4):
                    own, other = prob[:, u, t, P:], prob[:, u, t, :P]
                    if source == 0:
                        last = nc.tensor.transpose(o[:, 2 * t, :], own, ident[:, :])
                        if t < 3:
                            last = nc.tensor.transpose(o[:, 2 * t + 1, :], prob[:, u, t + 1, :P], ident[:, :])
                    else:
                        nc.tensor.transpose(o[:, 2 * t, :], other, ident[:, :])
                        last = nc.tensor.transpose(o[:, 2 * t + 1, :], own, ident[:, :])
                last.then_inc(turned, 1)

            def weigh(source, hh):
                o = bank[:, OB, :]
                hs = slice(hh * E, (hh + 1) * E)
                pt = probT[:, source, :].rearrange("p (c k) -> p c k", k=P)
                for t in range(4):
                    if source == 0:
                        n = min(2, 4 - t)
                        last = mm(o[:, t * P:(t + n) * P], v[:, 0, t, hs], probT[:, source, 2 * t * P:(2 * t + n) * P],
                                  start=t == 0, stop=False, skip_group_check=True)
                    else:
                        for g in (1, 2):
                            last = mm(o[:, t:S:NR], v[:, g, t, hs], pt[:, 2 * t + g - 1, :],
                                      start=False, stop=t == 3 and g == 2, skip_group_check=True)
                last.then_inc(summed, 1)

            def trade():
                o = bank[:, OB, 0:P].rearrange("p (s a h r t) -> p s a h r t", s=2, a=2, h=2, r=NR)
                for s in range(2):
                    for r in range(NR):
                        last = mm(o[:, s, :, :, r, :], repT[:, s, r, :], stats[:, 0, 1 - s, :, :], start=True, stop=True)
                last.then_inc(stats_sent, 1)

            def attend(pair, last_pair):
                free = bank_free(pair)
                project(1, pair, free)
                project(2, pair, free)
                for hh in range(2):
                    pe.wait_ge(rotated, pair * QT + 3 + hh)
                    scores(0, hh)
                for c in range(3, 7):
                    project(c, pair, free)
                for hh in range(2):
                    pe.wait_ge(rotated, pair * QT + 11 + hh)
                    pe.wait_ge(masked, pair * 4 + 1 + hh)
                    scores(1, hh)
                project(7, pair, free)
                pe.wait_ge(probs_ready, pair * 4 + 4)
                trade()
                project(8, pair, free)
                def turn_next(source, hh):
                    pe.wait_ge(scaled, pair * 4 + 2 * hh + source + 1)
                    turn(source, hh)

                def weigh_next(source, hh):
                    n = 2 * hh + source
                    pe.wait_ge(turned_act, pair * 4 + n + 1)
                    pe.wait_ge(turned_dve, pair * 4 + n + 1)
                    if n == 2:
                        pe.wait_ge(head_low, pair * 2 + 1)
                    weigh(source, hh)

                turn_next(0, 0)
                turn_next(1, 0)

                def rest():
                    weigh_next(0, 0)
                    turn_next(0, 1)
                    weigh_next(1, 0)
                    turn_next(1, 1)

                if last_pair:
                    pe.wait_ge(v_stored, pair * VT + VT)
                    project_out(0, range(0, 3))
                    rest()
                    project_out(0, range(3, 6))
                else:
                    def between():
                        pe.wait_ge(v_stored, pair * VT + VT)
                        rest()

                    project(0, pair + 1, bank_free_next(pair), between=between)
                weigh_next(0, 1)
                weigh_next(1, 1)

            def first_operands(k):
                if k in (0, KT // 2):
                    pe.wait_ge(first_low if k == 0 else low_ready, 1)
                pe.wait_ge(xl_ready, k + 1)

            project(0, 0, before=first_operands)
            pe.wait_ge(conv_in_s, 32)
            nc.tensor.transpose(bank[:, SB, 0:4 * FT], conv_rows[:, :], ident[0:4 * FT, 0:4 * FT]).then_inc(conv_turned, 1)
            def project_out(r, heads):
                b = Y_BANK[r]
                ts = slice(r * P, (r + 1) * P)
                if r == 3:
                    pe.wait_ge(z_ready, 2 * 2)
                for h in heads:
                    if r == 0:
                        pe.wait_ge(low_ready, QKV_CHUNKS + h // 2 + 1)
                        if h >= H - 2:
                            pe.wait_ge(head_low, h + 1)
                    if r >= 1 and h == H - 2:
                        turn_x1(r - 1)
                    w_h, w_l = rows(wh[h // 2][:, :])[:, h % 2, :], rows(wl[h // 2][:, :])[:, h % 2, :]
                    for st, w in ((oTh, w_h), (oTh, w_l), (oTl, w_h)):
                        for half in range(2):
                            last = mm(bank[:, b + half, :], st[:, h, ts], w[:, half * S:(half + 1) * S],
                                      start=h == 0 and w is w_h and st is oTh, stop=h == H - 1 and st is oTl)
                    if r == NR - 1 and h in (1, 3):
                        last.then_inc(out_used, 1)
                if h == H - 1:
                    last.then_inc(y_ready, 1)

            def turn_x1(r):
                o = bank[:, T_BANK[r]:T_BANK[r] + 2, :].rearrange("p a (k l) -> p (a k) l", l=P)
                pe.wait_ge(ln_done, 2 * (r + 1))
                if r >= 2:
                    pe.wait_ge(x1l_ready, r - 1)
                for k in range(KT):
                    last = nc.tensor.transpose(o[:, k, :], res[:, r, k * P:(k + 1) * P], ident[:, :])
                last.then_inc(x1_turned, 1)

            with pe.Fori(0, PAIRS - 1) as pair:
                attend(pair, False)
            attend(PAIRS - 1, True)
            project_out(0, range(6, H))
            for r in range(1, NR):
                project_out(r, range(H))

            def up(t, f, lo, hi):
                h3, l3, cs = cols(wh[t][:, :]), cols(wl[t][:, :]), slice(f * P, (f + 1) * P)
                return three(bank[:, (GATE_BANK, VAL_BANK)[t] + f, lo:hi],
                             [((h3[:, k, cs], l3[:, k, cs]), (xTh[:, k, lo:hi], xTl[:, k, lo:hi])) for k in range(KT)])

            pe.wait_ge(x1l_ready, NR - 1)
            for t in range(2):
                pe.wait_ge(low_ready, UP0 + t + 1)
                if t == 1:
                    turn_x1(NR - 1)
                    pe.wait_ge(z_ready, 2 * NR)
                for f in range(2):
                    up(t, f, 0, EARLY)
            pe.wait_ge(x1l_ready, NR)
            for t in range(2):
                for f in range(2):
                    up(t, f, EARLY, S).then_inc(val_ready if t else gate_ready, 1)
            with pe.Fori(1, UP_STEPS) as i:
                for t in range(2):
                    pe.wait_ge(low_ready, 2 * i + UP0 + t + 1)
                    for f in range(2):
                        up(t, f, 0, S).then_inc(val_ready if t else gate_ready, 1)

            def down(m, tiles, finish, halves=(0, 1)):
                s = down_slot(m)
                h_h, h_l = half_slot(xTh, m), half_slot(xTl, m)
                for r in tiles:
                    ts = slice(r * P, (r + 1) * P)
                    for k in range(2):
                        for hid, w in ((h_h, wh[s]), (h_h, wl[s]), (h_l, wh[s])):
                            for half in halves:
                                first = m == 0 and k == 0 and hid is h_h and w is wh[s]
                                last = mm(bank[:, 2 * r + half, :], hid[:, k, ts], rows(w[:, :])[:, k, half * S:(half + 1) * S],
                                          start=first, stop=finish and k == 1 and hid is h_l)
                return last

            def down_ready(m):
                pe.wait_ge(low_ready, DOWN0 + m + 1)
                pe.wait_ge(hl_ready, m + 1)

            for m in range(2):
                down_ready(m)
                down(m, range(2), False)
                if m == 0:
                    pe.wait_ge(hidden_ready, FT)
                down(m, range(2, NR), False).then_inc(down_used, 1)
            with pe.Fori(1, DOWN_LOOP // 2) as i:
                for t in range(2):
                    pe.wait_ge(low_ready, 2 * i + DOWN0 + t + 1)
                    pe.wait_ge(hl_ready, 2 * i + t + 1)
                    down(t + 2, range(NR), False).then_inc(down_used, 1)
            down_ready(DOWN_LOOP)
            down(DOWN_LOOP, range(NR), False).then_inc(down_used, 1)
            for r in range(NR - 1):
                for m in range(DOWN_TAIL, DOWN):
                    if r == 0:
                        down_ready(m)
                    last = down(m, [r], m == DOWN - 1)
                last.then_inc(y_ready, 1)
            for half in range(2):
                for m in range(DOWN_TAIL, DOWN):
                    last = down(m, [NR - 1], m == DOWN - 1, [half])
                last.then_inc(y_ready if half else y_half, 1)

        @block.scalar
        def _(sc):
            act_ = nc.scalar.activation

            def high(n_sem, count, src, dst):
                sc.wait_ge(n_sem, count)
                act_(dst[:, :], src, ACT.Copy).then_inc(high_ready, 1)

            def high_qkv(c, pair):
                high(raw_in[c % 3], pair * 48 + 16 * (c // 3 + 1), raw[:, c % 3, :], wh[c % 3])

            first = KT // 2 * CW
            sc.wait_ge(first_in, 16)
            act_(wh[0][:, 0:first], raw[:, 0, 0:first], ACT.Copy).then_inc(first_high, 1)
            for k in range(KT):
                sc.wait_ge(x_turned, k + 1)
                act_(xTh[:, k, :], bank[:, k, :], ACT.Copy).then_inc(xh_ready, 1)
                if k == 1:
                    sc.wait_ge(raw_in[0], 16)
                    act_(wh[0][:, first:], raw[:, 0, first:], ACT.Copy).then_inc(high_ready, 1)
            high_qkv(1, 0)
            high_qkv(2, 0)
            sc.wait_ge(conv_turned, 1)
            act_(convp[:, :], bank[:, SB, 0:4 * FT], ACT.Copy).then_inc(conv_ready, 1)

            def next_high(c, pair):
                g, j = CHUNKS[c % NC]
                if j < 2:
                    sc.wait_ge(qk_tile, (pair + c // NC) * QT + 2 * (c % NC) + 2)
                else:
                    sc.wait_ge(v_tile, pair * VT + 4 * (g + 1))
                high_qkv(c + 3, pair)

            def exps(u, pair):
                sc.wait_ge(shift_ready, pair * 4 + u + 1)
                for t in range(4):
                    lo = P if u < 2 and t == 0 else 0
                    c = 4 * (u % 2) + t
                    last = act_(prob[:, u, t, lo:], prob[:, u, t, lo:], ACT.Exp, bias=stats[:, 0, u // 2, 0, c:c + 1],
                                accum_out=stats[:, 0, u // 2, 1, c:c + 1])
                last.then_inc(probs_ready, 1)

            def store_v(g, tiles, pair):
                for i in tiles:
                    t = 4 * g + i
                    sc.wait_ge(v_tile, pair * VT + t + 1)
                    act_(v[:, g, i, :], bank[:, (QT + t) % 3, 0:CW], ACT.Copy).then_inc(v_stored, 1)

            next_high(0, 0)

            def attend(pair, last_pair):
                next_high(1, pair)
                next_high(2, pair)
                exps(0, pair)
                exps(1, pair)
                for c in range(3, 6):
                    next_high(c, pair)
                store_v(0, range(4), pair)
                next_high(6, pair)
                store_v(1, (0,), pair)
                exps(2, pair)
                store_v(1, (1, 2), pair)
                exps(3, pair)
                store_v(1, (3,), pair)
                next_high(7, pair)
                store_v(2, (0,), pair)
                sc.wait_ge(merge_step, pair * 7 + 4)
                act_(mweight[:, :, :, :], merge[:, 1:3, :, :], ACT.Exp).then_inc(mweight_ready, 1)
                store_v(2, (1, 2, 3), pair)
                next_high(8, pair)
                for n, (source, hh) in enumerate([(0, 0), (1, 0), (0, 1), (1, 1)]):
                    sc.wait_ge(turned, pair * 4 + n + 1)
                    if n >= 2:
                        sc.wait_ge(summed, pair * 4 + n - 1)
                    act_(probT[:, source, 0:S], bank[:, SB + 2 * source, :], ACT.Copy).then_inc(turned_act, 1)
                head(0, pair)
                if not last_pair:
                    next_high(9, pair)
                head(1, pair)

            def head(hh, pair):
                sc.wait_ge(summed, pair * 4 + 2 * hh + 2)
                act_(oTh[:, bass.ds(2 * pair + hh, 1), :], bank[:, OB:OB + 1, :], ACT.Copy).then_inc(head_high, 1)

            with sc.Fori(0, PAIRS - 1) as pair:
                attend(pair, False)
            attend(PAIRS - 1, True)
            high(raw_in[0], 16 * (QKV_CHUNKS // 3 + 1 + 0) + 16, raw[:, 0, :], wh[3])

            for r in range(NR):
                if r == NR - 1:
                    for t in range(2):
                        sc.wait_ge(out_used, t + 1)
                        high(ff_in[t], 16, raw[:, 2 - t, :], wh[t])
                sc.wait_ge(x1_turned, r + 1)
                act_(xTh[:, :, r * P:(r + 1) * P], bank[:, T_BANK[r]:T_BANK[r] + 2, :].rearrange("p a (k l) -> p (a k) l", l=P),
                     ACT.Copy).then_inc(x1h_ready, 1)

            def hidden_high(m):
                sc.wait_ge(hidden_ready, 2 * m + 2)
                act_(half_slot(xTh, m), hidden[:, 2 * m:2 * m + 2, :], ACT.Copy).then_inc(hh_ready, 1)

            def tap_two(i):
                for f in range(2):
                    sc.wait_ge(gate_ready, 2 * i + f + 1)
                    act_(cv[:, f, :], bank[:, GATE_BANK + f, :], ACT.Identity, scale=convp[:, bass.ds(2 * i + (2 * FT + f), 1)],
                         bias=convp[:, bass.ds(2 * i + (3 * FT + f), 1)]).then_inc(tap2, 1)

            def up_step(i):
                sc.wait_ge(gate_ready, 2 * i + 2)
                high(ff_in[0], 16 * i + 32, raw[:, 2, :], wh[0])
                for f in range(2):
                    sc.wait_ge(tap0, 2 * i + f + 1)
                    act_(act[:, f, :], cv[:, f, :], ACT.Silu).then_inc(gated, 1)
                sc.wait_ge(gated, 2 * i + 2)
                sc.wait_ge(val_ready, 2 * i + 2)
                high(ff_in[1], 16 * i + 32, raw[:, 1, :], wh[1])

            tap_two(0)
            with sc.Fori(0, UP_STEPS - 1) as i:
                up_step(i)
                tap_two(i + 1)
            hidden_high(0)
            hidden_high(1)
            up_step(UP_STEPS - 1)
            for m in range(2, DOWN):
                used = {DOWN_LOOP: None, 7: 5, 8: 4, 9: 5, 10: 6}.get(m, m - 2)
                if used is not None:
                    sc.wait_ge(down_used, used + 1)
                high(ff_in[m % 2], 16 * (UP_STEPS + m // 2 + 1), raw[:, 2 - m % 2, :], wh[down_slot(m)])
                hidden_high(m)

        @block.vector
        def _(dv):
            tt, ts_, stt = nc.vector.tensor_tensor, nc.vector.tensor_scalar, nc.vector.scalar_tensor_tensor

            def low(count, src, hi, dst):
                dv.wait_ge(high_ready, count)
                tt(dst[:, :], src, hi[:, :].bitcast(F32), ALU.subtract).then_inc(low_ready, 1)

            def low_qkv(c, pair):
                low(pair * NC + c + 1, raw[:, c % 3, :], wh[c % 3], wl[c % 3])

            first = KT // 2 * CW
            dv.wait_ge(first_high, 1)
            tt(wl[0][:, 0:first], raw[:, 0, 0:first], wh[0][:, 0:first].bitcast(F32), ALU.subtract).then_inc(first_low, 1)
            for k in range(KT):
                dv.wait_ge(xh_ready, k + 1)
                tt(xTl[:, k, :], bank[:, k, :], xTh[:, k, :].bitcast(F32), ALU.subtract).then_inc(xl_ready, 1)
                if k == 2:
                    dv.wait_ge(high_ready, 1)
                    tt(wl[0][:, first:], raw[:, 0, first:], wh[0][:, first:].bitcast(F32), ALU.subtract).then_inc(low_ready, 1)
            low_qkv(1, 0)
            low_qkv(2, 0)
            dv.wait_ge(const_in_s, 16)
            dv.wait_ge(conv_ready, 1)

            def rope(c, pair, heads=(0, 1)):
                g, j = CHUNKS[c]
                for hh in heads:
                    t = 2 * c + hh
                    b = bank[:, t % 3, :]
                    dv.wait_ge(qk_tile, pair * QT + t + 1)
                    if t >= 2:
                        dv.wait_ge(rotated, pair * QT + t - 1)
                    by_cos, bc, cc = qk[:, g % 2, j, hh:hh + 1, :], bank[:, t % 3:t % 3 + 1, :], cosT.rearrange("p (o n) -> p o n", o=1)
                    if g > 0:
                        by_cos, bc, cc = tiles(by_cos), natural(bc), natural(cc)
                    tt(by_cos, bc, cc, ALU.mult)
                    tt(swapped[64:128, hh, :], b[0:64, :], sinT[0:64, :], ALU.mult)
                    tt(swapped[0:64, hh, :], b[64:128, :], sinT[64:128, :], ALU.mult).then_inc(rope_terms, 1)

            def mask(source, pair):
                for hh in range(2):
                    u = 2 * source + hh
                    dv.wait_ge(scores_ready, pair * 4 + u + 1)
                    ps = bank[:, SB + 2 * hh:SB + 2 * hh + 2, :].rearrange("p a (c k) -> p (a c) k", k=CW)
                    m = maskT[:, source:source + 1, :]
                    t0 = 1 - source
                    if source == 0:
                        stt(prob[:, u, 0, P:], ps[:, 0, P:], SCALE, maskT[:, 0, P:], ALU.mult, ALU.add)
                    stt(prob[:, u, t0:, :], ps[:, t0:, :], SCALE, m.broadcast_to([P, 4 - t0, CW]), ALU.mult, ALU.add).then_inc(masked, 1)
                for hh in range(2):
                    u = 2 * source + hh
                    c = 4 * hh
                    t0 = 1 - source
                    dv.wait_ge(masked, pair * 4 + u + 1)
                    if source == 0:
                        nc.vector.tensor_reduce(stats[:, 0, source, 0, c:c + 1], prob[:, u, 0, P:], X, ALU.max, negate=True)
                    nc.vector.tensor_reduce(stats[:, 0, source, 0, c + t0:c + 4], prob[:, u, t0:, :], X, ALU.max, negate=True).then_inc(shift_ready, 1)

            def merge_sources(pair):
                step = [0]

                def link(ins):
                    step[0] += 1
                    ins.then_inc(merge_step, 1)
                    dv.wait_ge(merge_step, pair * 7 + step[0])

                dv.wait_ge(stats_sent, pair + 1)
                ex = bank[:, OB, 0:P].rearrange("p (s x t) -> p s x t", s=2, t=NR)
                link(tt(picked[:, :, :].rearrange("p (s x) t -> p s x t", s=2), ex, selT.broadcast_to([P, 2, 16, NR]), ALU.mult))
                link(nc.vector.tensor_reduce(stats[:, 1, :, :, :].rearrange("p s a c -> p (s a c)"), picked[:, :, :], X, ALU.add))
                link(tt(merge[:, 0, :, :], stats[:, 0, :, 0, :], stats[:, 1, :, 0, :], ALU.min))
                link(tt(merge[:, 1:3, :, :], merge[:, 0:1, :, :].broadcast_to([P, 2, 2, 8]), stats[:, :, :, 0, :], ALU.subtract))
                dv.wait_ge(mweight_ready, pair + 1)
                link(tt(merge[:, 3:5, :, :], mweight[:, :, :, :], stats[:, :, :, 1, :], ALU.mult))
                link(tt(merge[:, 0, :, :], merge[:, 3, :, :], merge[:, 4, :, :], ALU.add))
                link(nc.vector.reciprocal(merge[:, 3, :, :], merge[:, 0, :, :]))
                tt(coef[:, :, :], mweight[:, 0, :, :], merge[:, 3, :, :], ALU.mult).then_inc(coef_ready, 1)

            def scale(pair):
                dv.wait_ge(coef_ready, pair + 1)
                for source, hh in ((0, 0), (1, 0), (0, 1), (1, 1)):
                    u = 2 * source + hh
                    for t in range(4):
                        lo = P if source == 0 and t == 0 else 0
                        c = 4 * hh + t
                        last = ts_(prob[:, u, t, lo:], prob[:, u, t, lo:], coef[:, source, c:c + 1], None, ALU.mult)
                    last.then_inc(scaled, 1)

            rope(0, 0)
            low_qkv(3, 0)

            def attend(pair, last_pair):
                rope(1, pair)
                low_qkv(4, pair)
                rope(2, pair)
                low_qkv(5, pair)
                mask(0, pair)
                for c in range(3, 6):
                    rope(c, pair)
                    low_qkv(c + 3, pair)
                low_qkv(9, pair)
                mask(1, pair)
                low_qkv(10, pair)
                merge_sources(pair)
                scale(pair)
                low_qkv(11, pair)
                def store_turned(n, source):
                    dv.wait_ge(turned, pair * 4 + n + 1)
                    if n >= 2:
                        dv.wait_ge(summed, pair * 4 + n - 1)
                    w = S if source else 3 * P
                    nc.vector.tensor_copy(probT[:, source, S:S + w], bank[:, SB + 2 * source + 1, 0:w]).then_inc(turned_dve, 1)

                store_turned(0, 0)
                store_turned(1, 1)
                if not last_pair:
                    rope(0, pair + 1, (0,))
                store_turned(2, 0)
                store_turned(3, 1)
                head(0, pair)
                if not last_pair:
                    rope(0, pair + 1, (1,))
                    low_qkv(12, pair)
                head(1, pair)

            def head(hh, pair):
                dv.wait_ge(head_high, pair * 2 + hh + 1)
                h = bass.ds(2 * pair + hh, 1)
                tt(oTl[:, h, :], bank[:, OB:OB + 1, :], oTh[:, h, :].bitcast(F32), ALU.subtract).then_inc(head_low, 1)

            with dv.Fori(0, PAIRS - 1) as pair:
                attend(pair, False)
            attend(PAIRS - 1, True)
            low(UP0, raw[:, 0, :], wh[3], wl[3])

            def layer_norm(i, r):
                n = NR * i + r
                b = (Y_BANK[r], 2 * r)[i]
                halves = [slice(0, S), slice(S, D)]
                if n >= 1:
                    dv.wait_ge(ln_done, 2 * n)
                for half, hs in enumerate(halves):
                    if n == 2 * NR - 1 and half == 0:
                        dv.wait_ge(y_half, 1)
                    else:
                        dv.wait_ge(y_ready, n + 1)
                    stt(zrow[:, hs], res[:, r, hs], ALPHA, bank[:, b + half, :], ALU.mult, ALU.add).then_inc(z_ready, 1)
                    if n == 2 * NR - 1 and half == 0:
                        dv.wait_ge(z_ready, 2 * n + 1)
                        nc.vector.bn_stats(small[:, 0:6], zrow[:, hs])
                for half, hs in enumerate(halves):
                    if n == 2 * NR - 1 and half == 0:
                        continue
                    dv.wait_ge(z_ready, 2 * n + 1 + half)
                    last = nc.vector.bn_stats(small[:, 6 * half:6 * half + 6], zrow[:, hs])
                last.then_inc(ln_stats, 1)
                dv.wait_ge(ln_stats, 3 * n + 1)
                nc.vector.bn_aggr(small[:, 12:14], small[:, 0:12]).then_inc(ln_stats, 1)
                dv.wait_ge(ln_stats, 3 * n + 2)
                nc.vector.tensor_scalar_add(small[:, 13:14], small[:, 13:14], EPS).then_inc(ln_stats, 1)
                if r == 0:
                    dv.wait_ge(ln_in, 32 * i + 32)
                for hs in halves:
                    stt(zrow[:, hs], zrow[:, hs], small[:, 12:13], lnp[:, 0, hs], ALU.subtract, ALU.mult).then_inc(centred, 1)
                dv.wait_ge(rstd_ready, n + 1)
                for half, hs in enumerate(halves):
                    dv.wait_ge(centred, 2 * n + half + 1)
                    stt(res[:, r, hs], zrow[:, hs], small[:, 14:15], lnp[:, 1, hs], ALU.mult, ALU.add).then_inc(ln_done, 1)

            def x1_low(r):
                ts = slice(r * P, (r + 1) * P)
                dv.wait_ge(x1h_ready, r + 1)
                tt(xTl[:, :, ts], bank[:, T_BANK[r]:T_BANK[r] + 2, :].rearrange("p a (k l) -> p (a k) l", l=P), xTh[:, :, ts].bitcast(F32),
                   ALU.subtract).then_inc(x1l_ready, 1)

            dv.wait_ge(res_in, 16)
            for r in range(NR):
                layer_norm(0, r)
                if 1 <= r < NR - 1:
                    x1_low(r - 1)
                if r == NR - 2:
                    for t in range(2):
                        low(UP0 + t + 1, raw[:, 2 - t, :], wh[t], wl[t])
                    x1_low(r)
            x1_low(NR - 1)

            def up_step(i):
                for f in range(2):
                    dv.wait_ge(tap2, 2 * i + f + 1)
                    stt(cv[:, f, 1:], bank[:, GATE_BANK + f, 0:S - 1], convp[:, bass.ds(2 * i + (FT + f), 1)], cv[:, f, 1:],
                        ALU.mult, ALU.add).then_inc(tap1, 1)
                for f in range(2):
                    dv.wait_ge(tap1, 2 * i + f + 1)
                    stt(cv[:, f, 2:], bank[:, GATE_BANK + f, 0:S - 2], convp[:, bass.ds(2 * i + f, 1)], cv[:, f, 2:],
                        ALU.mult, ALU.add).then_inc(tap0, 1)
                low(2 * i + UP0 + 3, raw[:, 2, :], wh[0], wl[0])
                for f in range(2):
                    dv.wait_ge(gated, 2 * i + f + 1)
                    dv.wait_ge(val_ready, 2 * i + f + 1)
                    tt(hidden[:, bass.ds(2 * i + f, 1), :], act[:, f:f + 1, :], bank[:, VAL_BANK + f:VAL_BANK + f + 1, :],
                       ALU.mult).then_inc(hidden_ready, 1)
                low(2 * i + UP0 + 4, raw[:, 1, :], wh[1], wl[1])

            def hidden_low(m):
                dv.wait_ge(hh_ready, m + 1)
                tt(half_slot(xTl, m), hidden[:, 2 * m:2 * m + 2, :], half_slot(xTh, m).bitcast(F32), ALU.subtract).then_inc(hl_ready, 1)

            with dv.Fori(0, UP_STEPS - 1) as i:
                up_step(i)
            hidden_low(0)
            hidden_low(1)
            up_step(UP_STEPS - 1)
            for m in range(2, DOWN):
                s = down_slot(m)
                low(DOWN0 + m + 1, raw[:, 2 - m % 2, :], wh[s], wl[s])
                hidden_low(m)
            for r in range(NR):
                layer_norm(1, r)

        @block.gpsimd
        def _(pool):
            def add_terms(c, pair):
                g, j = CHUNKS[c]
                for hh in range(2):
                    pool.wait_ge(rope_terms, pair * QT + 2 * c + hh + 1)
                    a, b = qk[:, g % 2, j, hh:hh + 1, :], swapped[:, hh:hh + 1, :]
                    if g > 0:
                        a, b = tiles(a), natural(b)
                    nc.gpsimd.tensor_tensor(a, a, b, ALU.add).then_inc(rotated, 1)

            nc.gpsimd.memset(small[:, 16:17], -0.5).then_inc(exponent, 1)
            add_terms(0, 0)

            def attend(pair, last_pair):
                for c in range(1, 6):
                    add_terms(c, pair)
                if not last_pair:
                    add_terms(0, pair + 1)

            with pool.Fori(0, PAIRS - 1) as pair:
                attend(pair, False)
            attend(PAIRS - 1, True)

            pool.wait_ge(exponent, 1)
            for n in range(2 * NR):
                pool.wait_ge(ln_stats, 3 * n + 3)
                nc.gpsimd.tensor_tensor(small[:, 14:15], small[:, 13:14], small[:, 16:17], ALU.pow).then_inc(rstd_ready, 1)


def kernel(x, attn_w_in, attn_w_out, ffn_w_up, ffn_conv_w, ffn_conv_b, ffn_w_down, ln_g, ln_b, **unused):
    import concourse.bacc as bacc
    from concourse.bass_utils import run_bass_kernel_spmd

    nc = bacc.Bacc("TRN2", target_bir_lowering=False, num_devices=1)
    arrays = {
        "x": x, "w_in": attn_w_in, "w_out": attn_w_out, "w_up": ffn_w_up, "conv_w": ffn_conv_w,
        "conv_b": ffn_conv_b, "w_down": ffn_w_down, "ln_g": ln_g, "ln_b": ln_b,
        "ident": np.eye(P, dtype=np.float32), "const": constants(),
    }
    arrays = {n: np.ascontiguousarray(a) for n, a in arrays.items()}
    args = [nc.dram_tensor(f"in_{n}", a.shape, F32, kind="ExternalInput").ap() for n, a in arrays.items()]
    out = nc.dram_tensor("out", (1, S, D), F32, kind="ExternalOutput").ap()
    layer(nc, *args, out)
    r = run_bass_kernel_spmd(nc, [{f"in_{n}": a for n, a in arrays.items()}], core_ids=[0])
    return r.results[0]["out"]
```

```python
import math
from contextlib import ExitStack

import numpy as np

import concourse.bass as bass
from concourse import mybir

F32 = mybir.dt.float32
F32R = mybir.dt.float32r
ALU = mybir.AluOpType
ACT = mybir.ActivationFunctionType
X = mybir.AxisListType.X

P = 128
S = 512
D = 1024
KT = D // P
NR = 4
G = 3
H = 8
E = 128
PAIRS = H // 2
FF = 2816
FT = FF // P
CONV = 3
CW = 256
ALPHA = 2.0 ** 0.25
EPS = 1e-5
WARM = 5
Y_BANK = (0, 4, 6, 4)
T_BANK = (2, 0, 2, 0)
GATE_BANK, VAL_BANK = 6, 4
SECOND_BANK = 2
EARLY = 2 * P
SCALE = E ** -0.5
NEG = -1e30

CHUNKS = [(g, j) for g in range(G) for j in (0, 1)] + [(g, 2) for g in range(G)]
NC = len(CHUNKS)
QT = 12
VT = 12
OUT_CHUNKS = 4
QKV_CHUNKS = PAIRS * NC
UP0 = QKV_CHUNKS + OUT_CHUNKS
UP_STEPS = FT // 2
DOWN0 = UP0 + 2 * UP_STEPS
DOWN = FT // 2
DOWN_LOOP = 6
DOWN_TAIL = 7

C_COS, C_SIN, C_MASK, C_REP = 0, S, 2 * S, 2 * S + 512
C_SPLIT = C_REP + 2 * P
C_SEL = C_SPLIT + 2 * 4 * NR
C_ALL = C_SEL + 2 * NR


def constants():
    pos = np.arange(S, dtype=np.float32)
    inv = (np.float32(10000.0) ** (-np.arange(0, E, 2, dtype=np.float32) / np.float32(E))).astype(np.float32)
    ang = (inv[:, None] * pos[None, :]).astype(np.float32)
    out = np.zeros((P, C_ALL), np.float32)
    out[:64, C_COS:C_COS + S] = out[64:, C_COS:C_COS + S] = np.cos(ang.astype(np.float64))
    sin = np.sin(ang.astype(np.float64))
    out[:64, C_SIN:C_SIN + S], out[64:, C_SIN:C_SIN + S] = sin, -sin
    q, k = np.arange(P)[:, None], np.arange(P)[None, :]
    mask = np.full((P, 2, CW), NEG, np.float32)
    mask[:, 0, :P][k >= q] = 0
    mask[:, 0, P:][k <= q] = 0
    mask[:, 1, :P][k <= q] = 0
    mask[:, 1, P:][(k <= q) & ((q - k) % 4 == 0)] = 0
    out[:, C_MASK:C_MASK + 512] = mask.reshape(P, 512)
    rep, split, sel = np.zeros((P, 2, P), np.float32), np.zeros((P, 2, 4, NR), np.float32), np.zeros((P, 2, NR), np.float32)
    p = np.arange(P)
    for m in range(NR):
        rep[32 * m + p // 4, 0, p] = 1
        rep[4 * (p % 32) + m, 1, p] = 1
        split[p // 32 == m, 0, :, m] = 1
        split[p % 4 == m, 1, :, m] = 1
    sel[p, 0, p % 4] = 1
    sel[p, 1, p // 32] = 1
    out[:, C_REP:C_REP + 2 * P] = rep.reshape(P, 2 * P)
    out[:, C_SPLIT:C_SPLIT + 32] = split[:, ::-1].reshape(P, 32)
    out[:, C_SEL:C_SEL + 8] = sel.reshape(P, 8)
    return out


def layer(nc, x, w_in, w_out, w_up, conv_w, conv_b, w_down, ln_g, ln_b, ident_in, const_in, out):
    es = ExitStack()
    with es:
        def sb(name, shape, dt=F32, scope=es):
            return scope.enter_context(nc.sbuf_tensor(name, shape, dt))

        def sem(name):
            return es.enter_context(nc.semaphore(name))

        raw = sb("raw", [P, 3, KT * CW])
        wh = [sb(f"wh{s}", [P, KT * CW], F32R) for s in range(3)]
        wl = [sb(f"wl{s}", [P, KT * CW], F32R) for s in range(3)]
        xTh = sb("xTh", [P, KT, S], F32R)
        xTl = sb("xTl", [P, KT, S], F32R)
        ident = sb("ident", [P, P])
        convp = sb("convp", [P, 4 * FT])
        small = sb("small", [P, 64])
        with ExitStack() as s0:
            x_rows = sb("x_rows", [P, NR, D], scope=s0)
            conv_rows = sb("conv_rows", [4 * FT, P], scope=s0)
            zeros = sb("zeros", [P, CW], scope=s0)
        with ExitStack() as s1:
            qk = sb("qk", [P, 2, 2, 2, S], scope=s1)
            v = sb("v", [P, G, NR, CW], scope=s1)
            prob = sb("prob", [P, 4, NR, CW], scope=s1)
            probT = sb("probT", [P, 2, 8 * P], scope=s1)
            swapped = sb("swapped", [P, 2, S], scope=s1)
            oTh = sb("oTh", [P, H, S], F32R, scope=s1)
            oTl = sb("oTl", [P, H, S], F32R, scope=s1)
            const = sb("const", [P, C_ALL], scope=s1)
            stats = sb("stats", [P, 2, 2, 2, 8], scope=s1)
            spread = sb("spread", [P, 8, NR, NR], scope=s1)
            picked = sb("picked", [P, 32, NR], scope=s1)
            merge = sb("merge", [P, 5, 2, 8], scope=s1)
            coef = sb("coef", [P, 2, 8], scope=s1)
            mweight = sb("mweight", [P, 2, 2, 8], scope=s1)
        with ExitStack() as s2:
            res = sb("res", [P, NR, D], scope=s2)
            lnp = sb("lnp", [P, 2, D], scope=s2)
            zrow = sb("zrow", [P, D], scope=s2)
            wh.append(sb("wh3", [P, KT * CW], F32R, scope=s2))
            wl.append(sb("wl3", [P, KT * CW], F32R, scope=s2))
            hidden = sb("hidden", [P, FT, S], scope=s2)
            cv = sb("cv", [P, 2, S], scope=s2)
            act = sb("act", [P, 2, S], scope=s2)
        bank = es.enter_context(nc.psum_tensor("bank", [P, 8, S], F32))
        OB, SB = 3, 4

        cosT, sinT = const[:, C_COS:C_COS + S], const[:, C_SIN:C_SIN + S]
        maskT = const[:, C_MASK:C_MASK + 512].rearrange("p (s k) -> p s k", s=2)
        repT = const[:, C_REP:C_REP + 2 * P].rearrange("p (s k) -> p s k", s=2)
        splitT = const[:, C_SPLIT:C_SPLIT + 32].rearrange("p (x r o) -> p x r o", r=NR, o=1)
        selT = const[:, C_SEL:C_SEL + 8].rearrange("p (s o t) -> p s o t", s=2, o=1)

        ident_in_s, const_in_s, conv_in_s = sem("ident_loaded"), sem("const_loaded"), sem("conv_loaded")
        x_in_s = [sem(f"x_loaded{q}") for q in range(4)]
        raw_in = [sem(f"raw_loaded{s}") for s in range(3)]
        ff_in = [sem(f"ff_loaded{s}") for s in range(2)]
        high_ready, low_ready = sem("high_ready"), sem("low_ready")
        out_used, down_used = sem("out_used"), sem("down_used")
        x_turned, xh_ready, xl_ready = sem("x_turned"), sem("xh_ready"), sem("xl_ready")
        conv_turned, conv_ready = sem("conv_turned"), sem("conv_ready")
        qk_tile, v_tile = sem("qk_tile"), sem("v_tile")
        rope_terms, rotated = sem("rope_terms"), sem("rotated")
        v_stored = sem("v_stored")
        scores_ready, masked, shift_ready = sem("scores_ready"), sem("masked"), sem("shift_ready")
        probs_ready, spread_ready, stats_sent, merge_step = sem("probs_ready"), sem("spread_ready"), sem("stats_sent"), sem("merge_step")
        mweight_ready, coef_ready, scaled = sem("mweight_ready"), sem("coef_ready"), sem("scaled")
        turned, turned_act, turned_dve = sem("turned"), sem("turned_act"), sem("turned_dve")
        summed, head_high, head_low = sem("summed"), sem("head_high"), sem("head_low")
        res_in, ln_in = sem("res_loaded"), sem("ln_loaded")
        y_ready, y_half = sem("y_ready"), sem("y_half")
        z_ready, ln_stats, rstd_ready, centred, ln_done = sem("z_ready"), sem("ln_stats"), sem("rstd_ready"), sem("centred"), sem("ln_done")
        first_in, first_high, first_low = sem("first_loaded"), sem("first_high"), sem("first_low")
        x1_turned, x1h_ready, x1l_ready = sem("x1_turned"), sem("x1h_ready"), sem("x1l_ready")
        gate_ready, tap2, tap1, tap0 = sem("gate_ready"), sem("tap2"), sem("tap1"), sem("tap0")
        val_ready, gated, hidden_ready = sem("val_ready"), sem("gated"), sem("hidden_ready")
        hh_ready, hl_ready = sem("hh_ready"), sem("hl_ready")
        zeros_ready = sem("zeros_ready")
        exponent, stored = sem("exponent"), sem("stored")
        block = es.enter_context(nc.Block())

        w_in_v = w_in[0].rearrange("(k p) n -> p k n", p=P)
        w_up_v = w_up[0].rearrange("(k p) n -> p k n", p=P)
        w_out_v = w_out[0].rearrange("(k p) n -> p k n", p=P)
        w_down_v = w_down[0].rearrange("(k p) n -> p k n", p=P)
        x_blocks = x[0].rearrange("(b p) d -> p b d", p=P)
        out_blocks = out[0].rearrange("(b p) d -> p b d", p=P)

        def cols(chunk):
            return chunk.rearrange("p (k n) -> p k n", k=KT)

        def rows(chunk):
            return chunk.rearrange("p (k n) -> p k n", k=2)

        def natural(t):
            return t.rearrange("p a (l r) -> p a l r", r=NR)

        def tiles(t):
            return t.rearrange("p a (r l) -> p a l r", r=NR)

        def half_slot(t, m):
            if m < DOWN_LOOP:
                return (wh if t is xTh else wl)[3][:, (m % 2) * 2 * S:(m % 2 + 1) * 2 * S].rearrange("p (k n) -> p k n", k=2)
            j = (m - DOWN_LOOP) % 4
            return t[:, 2 * j:2 * j + 2, :]

        def down_slot(m):
            return m % 2 if m < DOWN_LOOP else (2, 3, 0, 1, 2)[m - DOWN_LOOP]

        @block.sync
        def _(sp):
            def load_qkv(c, col, n):
                sp.dma_start(cols(raw[:, n % 3, :]), w_in_v[:, :, bass.ds(col, CW)]).then_inc(raw_in[n % 3], 16)

            def column(c, pair):
                g, j = CHUNKS[c]
                return (g * 3 + j) * H * E + pair * CW

            half, c0 = KT // 2, column(0, 0)
            def load_x(q):
                sp.dma_start(x_rows[:, :, q * CW:(q + 1) * CW], x_blocks[:, :, q * CW:(q + 1) * CW]).then_inc(x_in_s[q], 16)

            sp.dma_start(cols(raw[:, 0, :])[:, :half, :], w_in_v[:, :half, c0:c0 + CW]).then_inc(first_in, 16)
            sp.dma_start(ident[:, :], ident_in).then_inc(ident_in_s, 16)
            load_x(0)
            load_x(1)
            sp.dma_start(cols(raw[:, 0, :])[:, half:, :], w_in_v[:, half:, c0:c0 + CW]).then_inc(raw_in[0], 16)
            load_x(2)
            load_x(3)
            load_qkv(1, column(1, 0), 1)
            sp.dma_start(const[:, :], const_in).then_inc(const_in_s, 16)
            load_qkv(2, column(2, 0), 2)
            sp.dma_start(conv_rows[0:CONV * FT, :], conv_w[0].rearrange("t (f p) -> (t f) p", p=P)).then_inc(conv_in_s, 16)
            sp.dma_start(conv_rows[CONV * FT:, :], conv_b[0].rearrange("(f p) -> f p", p=P)).then_inc(conv_in_s, 16)
            sp.wait_ge(low_ready, 1)
            load_qkv(3, column(3, 0), 3)

            def loads(pair, last):
                for c in range(1, NC + 1):
                    sp.wait_ge(low_ready, pair * NC + c + 1)
                    n = c + 3
                    if n < NC:
                        load_qkv(n, column(n, pair), n)
                    elif not last:
                        load_qkv(n - NC, column(n - NC, pair + 1), n)
                    else:
                        k = n - NC
                        sp.dma_start(rows(raw[:, n % 3, :]), w_out_v[:, 2 * k:2 * k + 2, :]).then_inc(raw_in[n % 3], 16)

            with sp.Fori(0, PAIRS - 1) as pair:
                loads(pair, False)
            loads(PAIRS - 1, True)

            sp.wait_ge(scores_ready, 4 * PAIRS)
            sp.dma_start(res[:, :, :], x_blocks).then_inc(res_in, 16)
            sp.wait_ge(summed, 4 * PAIRS)

            def load_ln(i):
                sp.dma_start(lnp[:, 0, :], ln_g[0, i:i + 1, :].broadcast_to([P, D])).then_inc(ln_in, 16)
                sp.dma_start(lnp[:, 1, :], ln_b[0, i:i + 1, :].broadcast_to([P, D])).then_inc(ln_in, 16)

            load_ln(0)

            def load_up(i, t):
                slot = 2 - t
                sp.dma_start(cols(raw[:, slot, :]), w_up_v[:, :, bass.ds(i * CW + t * FF, CW)]).then_inc(ff_in[t], 16)

            def load_down(m):
                t = m % 2
                sp.dma_start(rows(raw[:, 2 - t, :]), w_down_v[:, 2 * m:2 * m + 2, :]).then_inc(ff_in[t], 16)

            sp.wait_ge(low_ready, UP0 - 1)
            load_up(0, 0)
            load_up(0, 1)
            with sp.Fori(1, UP_STEPS) as i:
                sp.wait_ge(low_ready, UP0 - 1 + 2 * i)
                load_up(i, 0)
                sp.wait_ge(low_ready, UP0 + 2 * i)
                load_up(i, 1)
            for m in range(DOWN):
                sp.wait_ge(low_ready, DOWN0 + m - 1)
                load_down(m)
                if m == 0:
                    sp.wait_ge(ln_done, 2 * NR)
                    load_ln(1)
            for r in range(NR - 1):
                sp.wait_ge(ln_done, 2 * (NR + r + 1))
                sp.dma_start(out_blocks[:, r, :], res[:, r, :]).then_inc(stored, 16)
            for half in range(2):
                sp.wait_ge(ln_done, 4 * NR - 1 + half)
                hs = slice(half * S, (half + 1) * S)
                sp.dma_start(out_blocks[:, NR - 1, hs], res[:, NR - 1, hs]).then_inc(stored, 16)
            sp.wait_ge(stored, 16 * (NR + 1))

        @block.tensor
        def _(pe):
            mm = nc.tensor.matmul

            def three(o, pairs):
                n = len(pairs)
                for i, ((sh, sl), (mh, ml)) in enumerate(pairs):
                    mm(o, sh, mh, start=i == 0, stop=False)
                    mm(o, sh, ml, start=False, stop=False)
                    last = mm(o, sl, mh, start=False, stop=i == n - 1)
                return last

            pe.wait_ge(zeros_ready, 1)
            for _ in range(WARM):
                mm(bank[:, KT - 1, 0:CW], zeros[:, 0:P], zeros[:, 0:CW], start=True, stop=True)

            pe.wait_ge(ident_in_s, 16)

            def turn_x(k):
                if k % 2 == 0:
                    pe.wait_ge(x_in_s[k // 2], 16)
                for r in range(NR):
                    t = nc.tensor.transpose(bank[:, k, r * P:(r + 1) * P], x_rows[:, r, k * P:(k + 1) * P], ident[:, :])
                t.then_inc(x_turned, 1)

            def project(c, pair, free, between=None):
                g, j = CHUNKS[c]
                h3, l3 = cols(wh[c % 3][:, :]), cols(wl[c % 3][:, :])
                pe.wait_ge(low_ready, pair * NC + c + 1)
                if j < 2:
                    for hh in range(2):
                        t = 2 * c + hh
                        free(t)
                        cs = slice(hh * E, (hh + 1) * E)
                        last = three(bank[:, t % 3, :], [((h3[:, k, cs], l3[:, k, cs]), (xTh[:, k, :], xTl[:, k, :])) for k in range(KT)])
                        if hh == 0:
                            last.then_inc(qk_tile, 1)
                            if between:
                                between()
                    last.then_inc(qk_tile, 1)
                else:
                    for i in range(NR):
                        t = QT + 4 * g + i
                        free(t)

                        def tok(a, k):
                            return a[:, k, i * P:(i + 1) * P] if g == 0 else a[:, k, i:S:NR]

                        last = three(bank[:, t % 3, 0:CW], [((tok(xTh, k), tok(xTl, k)), (h3[:, k, :], l3[:, k, :])) for k in range(KT)])
                        if i < NR - 1:
                            last.then_inc(v_tile, 1)
                        if i == 0 and between:
                            between()
                    last.then_inc(v_tile, 1)

            def bank_free(pair):
                def free(t):
                    if t >= QT + 3:
                        pe.wait_ge(v_stored, pair * VT + t - QT - 2)
                    elif t >= 3:
                        pe.wait_ge(rope_terms, pair * QT + t - 2)
                return free

            def bank_free_next(pair):
                return lambda t: pe.wait_ge(v_stored, pair * VT + VT - 2 + t)

            def scores(source, hh):
                u = 2 * source + hh
                o = bank[:, SB + 2 * (u % 2):SB + 2 * (u % 2) + 2, :].rearrange("p a (c k) -> p (a c) k", k=CW)
                for t in range(4):
                    if source == 0:
                        lo = max(t - 1, 0) * P
                        last = mm(o[:, t, (P if t == 0 else 0):], qk[:, 0, 0, hh, t * P:(t + 1) * P],
                                  qk[:, 0, 1, hh, lo:(t + 1) * P], start=True, stop=True)
                    else:
                        for g in (1, 2):
                            ts = slice(t * P, (t + 1) * P)
                            last = mm(o[:, t, (g - 1) * P:g * P], qk[:, g % 2, 0, hh, ts], qk[:, g % 2, 1, hh, ts],
                                      start=True, stop=True)
                last.then_inc(scores_ready, 1)

            def turn(source, hh):
                u = 2 * source + hh
                o = bank[:, SB + 2 * source:SB + 2 * source + 2, :].rearrange("p a (c k) -> p (a c) k", k=P)
                for t in range(4):
                    own, other = prob[:, u, t, P:], prob[:, u, t, :P]
                    if source == 0:
                        last = nc.tensor.transpose(o[:, 2 * t, :], own, ident[:, :])
                        if t < 3:
                            last = nc.tensor.transpose(o[:, 2 * t + 1, :], prob[:, u, t + 1, :P], ident[:, :])
                    else:
                        nc.tensor.transpose(o[:, 2 * t, :], other, ident[:, :])
                        last = nc.tensor.transpose(o[:, 2 * t + 1, :], own, ident[:, :])
                last.then_inc(turned, 1)

            def weigh(source, hh):
                o = bank[:, OB, :]
                hs = slice(hh * E, (hh + 1) * E)
                pt = probT[:, source, :].rearrange("p (c k) -> p c k", k=P)
                for t in range(4):
                    if source == 0:
                        n = min(2, 4 - t)
                        last = mm(o[:, t * P:(t + n) * P], v[:, 0, t, hs], probT[:, source, 2 * t * P:(2 * t + n) * P],
                                  start=t == 0, stop=False, skip_group_check=True)
                    else:
                        for g in (1, 2):
                            last = mm(o[:, t:S:NR], v[:, g, t, hs], pt[:, 2 * t + g - 1, :],
                                      start=False, stop=t == 3 and g == 2, skip_group_check=True)
                last.then_inc(summed, 1)

            def trade():
                for s in range(2):
                    last = mm(bank[:, OB, s * 64:(s + 1) * 64], repT[:, s, :], spread[:, 4 * (1 - s):4 * (2 - s), :, :], start=True, stop=True)
                last.then_inc(stats_sent, 1)

            def attend(pair, last_pair):
                free = bank_free(pair)
                project(1, pair, free)
                project(2, pair, free)
                for hh in range(2):
                    pe.wait_ge(rotated, pair * QT + 3 + hh)
                    scores(0, hh)
                for c in range(3, 7):
                    project(c, pair, free)
                for hh in range(2):
                    pe.wait_ge(rotated, pair * QT + 11 + hh)
                    pe.wait_ge(masked, pair * 4 + 1 + hh)
                    scores(1, hh)
                project(7, pair, free)

                def trade_now():
                    pe.wait_ge(spread_ready, pair + 1)
                    trade()

                project(8, pair, free, between=trade_now)
                def turn_next(source, hh):
                    pe.wait_ge(scaled, pair * 4 + 2 * hh + source + 1)
                    turn(source, hh)

                def weigh_next(source, hh):
                    n = 2 * hh + source
                    pe.wait_ge(turned_act, pair * 4 + n + 1)
                    pe.wait_ge(turned_dve, pair * 4 + n + 1)
                    if n == 2:
                        pe.wait_ge(head_low, pair * 2 + 1)
                    weigh(source, hh)

                turn_next(0, 0)
                turn_next(1, 0)

                def rest():
                    weigh_next(0, 0)
                    turn_next(0, 1)
                    weigh_next(1, 0)
                    turn_next(1, 1)

                if last_pair:
                    pe.wait_ge(v_stored, pair * VT + VT)
                    project_out(0, range(0, 3))
                    rest()
                    project_out(0, range(3, 6))
                else:
                    def between():
                        pe.wait_ge(v_stored, pair * VT + VT)
                        rest()

                    project(0, pair + 1, bank_free_next(pair), between=between)
                weigh_next(0, 1)
                weigh_next(1, 1)

            h3, l3 = cols(wh[0][:, :]), cols(wl[0][:, :])
            for k in range(4):
                turn_x(k)
            for k in range(KT):
                if k in (2, 4):
                    turn_x(k + 2)
                    turn_x(k + 3)
                if k in (0, KT // 2):
                    pe.wait_ge(first_low if k == 0 else low_ready, 1)
                pe.wait_ge(xl_ready, max(k + 1, 2))
                for w, a in ((h3, xTh), (h3, xTl), (l3, xTh)):
                    for hh in range(2):
                        last = mm(bank[:, hh, :], w[:, k, hh * E:(hh + 1) * E], a[:, k, :], start=k == 0 and a is xTh and w is h3,
                                  stop=k == KT - 1 and w is l3)
                        if k == KT - 1 and w is l3:
                            last.then_inc(qk_tile, 1)
            pe.wait_ge(conv_in_s, 32)
            nc.tensor.transpose(bank[:, SB, 0:4 * FT], conv_rows[:, :], ident[0:4 * FT, 0:4 * FT]).then_inc(conv_turned, 1)
            def project_out(r, heads):
                b = Y_BANK[r]
                ts = slice(r * P, (r + 1) * P)
                first, final = (4, 3) if r == NR - 1 else (0, H - 1)
                if r == 3:
                    pe.wait_ge(z_ready, 2 * 2)
                for n, h in enumerate(heads):
                    if r == 0:
                        pe.wait_ge(low_ready, QKV_CHUNKS + h // 2 + 1)
                        if h >= H - 2:
                            pe.wait_ge(head_low, h + 1)
                    if r >= 1 and n == H - 2:
                        turn_x1(r - 1)
                    w_h, w_l = rows(wh[h // 2][:, :])[:, h % 2, :], rows(wl[h // 2][:, :])[:, h % 2, :]
                    for st, w in ((oTh, w_h), (oTh, w_l), (oTl, w_h)):
                        for half in range(2):
                            last = mm(bank[:, b + half, :], st[:, h, ts], w[:, half * S:(half + 1) * S],
                                      start=h == first and w is w_h and st is oTh, stop=h == final and st is oTl)
                    if r == NR - 1 and n in (1, 3):
                        last.then_inc(out_used, 1)
                if h == final:
                    last.then_inc(y_ready, 1)

            def turn_x1(r):
                o = bank[:, T_BANK[r]:T_BANK[r] + 2, :].rearrange("p a (k l) -> p (a k) l", l=P)
                pe.wait_ge(ln_done, 2 * (r + 1))
                if r >= 2:
                    pe.wait_ge(x1l_ready, r - 1)
                for k in range(KT):
                    last = nc.tensor.transpose(o[:, k, :], res[:, r, k * P:(k + 1) * P], ident[:, :])
                last.then_inc(x1_turned, 1)

            with pe.Fori(0, PAIRS - 1) as pair:
                attend(pair, False)
            attend(PAIRS - 1, True)
            project_out(0, range(6, H))
            for r in range(1, NR - 1):
                project_out(r, range(H))
            project_out(NR - 1, [4, 5, 6, 7, 0, 1, 2, 3])

            def up(b, t, f, lo, hi, slot):
                h3, l3, cs = cols(wh[slot + t][:, :]), cols(wl[slot + t][:, :]), slice(f * P, (f + 1) * P)
                return three(bank[:, b + f, lo:hi], [((h3[:, k, cs], l3[:, k, cs]), (xTh[:, k, lo:hi], xTl[:, k, lo:hi])) for k in range(KT)])

            pe.wait_ge(x1l_ready, EARLY // P)
            for t, f in ((0, 0), (0, 1), (1, 0), (1, 1)):
                if f == 0:
                    pe.wait_ge(low_ready, UP0 + t + 1)
                if t == 1 and f == 0:
                    pe.wait_ge(z_ready, 2 * NR)
                if t == 1 and f == 1:
                    turn_x1(NR - 1)
                up((GATE_BANK, VAL_BANK)[t], t, f, 0, EARLY, 2)
            pe.wait_ge(low_ready, UP0 + 3)
            pe.wait_ge(x1l_ready, NR - 1)
            for f in range(2):
                up(SECOND_BANK, 0, f, 0, EARLY, 0)
            pe.wait_ge(x1l_ready, NR)
            for t in range(2):
                for f in range(2):
                    up((GATE_BANK, VAL_BANK)[t], t, f, EARLY, S, 2).then_inc(val_ready if t else gate_ready, 1)
            for f in range(2):
                up(SECOND_BANK, 0, f, EARLY, S, 0).then_inc(gate_ready, 1)
            pe.wait_ge(low_ready, UP0 + 4)
            for f in range(2):
                pe.wait_ge(hidden_ready, f + 1)
                up(VAL_BANK, 1, f, 0, S, 0).then_inc(val_ready, 1)
            with pe.Fori(2, UP_STEPS) as i:
                for t in range(2):
                    pe.wait_ge(low_ready, 2 * i + UP0 + t + 1)
                    for f in range(2):
                        pe.wait_ge(hidden_ready if t else tap0, 2 * i + (f - 1))
                        up((GATE_BANK, VAL_BANK)[t], t, f, 0, S, 0).then_inc(val_ready if t else gate_ready, 1)

            def down(m, tiles, finish, halves=(0, 1)):
                s = down_slot(m)
                h_h, h_l = half_slot(xTh, m), half_slot(xTl, m)
                for r in tiles:
                    ts = slice(r * P, (r + 1) * P)
                    for k in range(2):
                        for hid, w in ((h_h, wh[s]), (h_h, wl[s]), (h_l, wh[s])):
                            for half in halves:
                                first = m == 0 and k == 0 and hid is h_h and w is wh[s]
                                last = mm(bank[:, 2 * r + half, :], hid[:, k, ts], rows(w[:, :])[:, k, half * S:(half + 1) * S],
                                          start=first, stop=finish and k == 1 and hid is h_l)
                return last

            def down_ready(m):
                pe.wait_ge(low_ready, DOWN0 + m + 1)
                pe.wait_ge(hl_ready, m + 1)

            for m in range(2):
                down_ready(m)
                down(m, range(2), False)
                if m == 0:
                    pe.wait_ge(hidden_ready, FT)
                down(m, range(2, NR), False).then_inc(down_used, 1)
            with pe.Fori(1, DOWN_LOOP // 2) as i:
                for t in range(2):
                    pe.wait_ge(low_ready, 2 * i + DOWN0 + t + 1)
                    pe.wait_ge(hl_ready, 2 * i + t + 1)
                    down(t + 2, range(NR), False).then_inc(down_used, 1)
            down_ready(DOWN_LOOP)
            down(DOWN_LOOP, range(NR), False).then_inc(down_used, 1)
            for r in range(NR - 1):
                for m in range(DOWN_TAIL, DOWN):
                    if r == 0:
                        down_ready(m)
                    last = down(m, [r], m == DOWN - 1)
                last.then_inc(y_ready, 1)
            for half in range(2):
                for m in range(DOWN_TAIL, DOWN):
                    last = down(m, [NR - 1], m == DOWN - 1, [half])
                last.then_inc(y_ready if half else y_half, 1)

        @block.scalar
        def _(sc):
            act_ = nc.scalar.activation

            def high(n_sem, count, src, dst):
                sc.wait_ge(n_sem, count)
                act_(dst[:, :], src, ACT.Copy).then_inc(high_ready, 1)

            def high_qkv(c, pair):
                high(raw_in[c % 3], pair * 48 + 16 * (c // 3 + 1), raw[:, c % 3, :], wh[c % 3])

            first = KT // 2 * CW
            sc.wait_ge(first_in, 16)
            act_(wh[0][:, 0:first], raw[:, 0, 0:first], ACT.Copy).then_inc(first_high, 1)
            for k in range(KT):
                sc.wait_ge(x_turned, k + 1)
                act_(xTh[:, k, :], bank[:, k, :], ACT.Copy).then_inc(xh_ready, 1)
                if k == 1:
                    sc.wait_ge(raw_in[0], 16)
                    act_(wh[0][:, first:], raw[:, 0, first:], ACT.Copy).then_inc(high_ready, 1)
            high_qkv(1, 0)
            high_qkv(2, 0)
            sc.wait_ge(conv_turned, 1)
            act_(convp[:, :], bank[:, SB, 0:4 * FT], ACT.Copy).then_inc(conv_ready, 1)

            def next_high(c, pair):
                g, j = CHUNKS[c % NC]
                if j < 2:
                    sc.wait_ge(qk_tile, (pair + c // NC) * QT + 2 * (c % NC) + 2)
                else:
                    sc.wait_ge(v_tile, pair * VT + 4 * (g + 1))
                high_qkv(c + 3, pair)

            def exps(u, pair):
                sc.wait_ge(shift_ready, pair * 4 + u + 1)
                for t in range(4):
                    lo = P if u < 2 and t == 0 else 0
                    c = 4 * (u % 2) + t
                    last = act_(prob[:, u, t, lo:], prob[:, u, t, lo:], ACT.Exp, bias=stats[:, 0, u // 2, 0, c:c + 1],
                                accum_out=stats[:, 0, u // 2, 1, c:c + 1])
                last.then_inc(probs_ready, 1)

            def store_v(g, tiles, pair):
                for i in tiles:
                    t = 4 * g + i
                    sc.wait_ge(v_tile, pair * VT + t + 1)
                    act_(v[:, g, i, :], bank[:, (QT + t) % 3, 0:CW], ACT.Copy).then_inc(v_stored, 1)

            next_high(0, 0)

            def attend(pair, last_pair):
                next_high(1, pair)
                next_high(2, pair)
                exps(0, pair)
                exps(1, pair)
                for c in range(3, 6):
                    next_high(c, pair)
                store_v(0, range(4), pair)
                next_high(6, pair)
                store_v(1, (0,), pair)
                exps(2, pair)
                store_v(1, (1, 2), pair)
                exps(3, pair)
                store_v(1, (3,), pair)
                next_high(7, pair)
                store_v(2, (0,), pair)
                sc.wait_ge(merge_step, pair * 7 + 4)
                act_(mweight[:, :, :, :], merge[:, 1:3, :, :], ACT.Exp).then_inc(mweight_ready, 1)
                store_v(2, (1, 2, 3), pair)
                for n, (source, hh) in enumerate([(0, 0), (1, 0), (0, 1), (1, 1)]):
                    if n == 2:
                        next_high(8, pair)
                    sc.wait_ge(turned, pair * 4 + n + 1)
                    if n >= 2:
                        sc.wait_ge(summed, pair * 4 + n - 1)
                    act_(probT[:, source, 0:S], bank[:, SB + 2 * source, :], ACT.Copy).then_inc(turned_act, 1)
                head(0, pair)
                if last_pair:
                    high(raw_in[0], pair * 48 + 80, raw[:, 0, :], wh[3])
                else:
                    next_high(9, pair)
                head(1, pair)

            def head(hh, pair):
                sc.wait_ge(summed, pair * 4 + 2 * hh + 2)
                act_(oTh[:, bass.ds(2 * pair + hh, 1), :], bank[:, OB:OB + 1, :], ACT.Copy).then_inc(head_high, 1)

            with sc.Fori(0, PAIRS - 1) as pair:
                attend(pair, False)
            attend(PAIRS - 1, True)
            for r in range(NR):
                if r == NR - 2:
                    for t in range(2):
                        sc.wait_ge(out_used, t + 1)
                        high(ff_in[t], 16, raw[:, 2 - t, :], wh[2 + t])
                if r == NR - 1:
                    sc.wait_ge(y_ready, NR)
                    high(ff_in[0], 32, raw[:, 2, :], wh[0])
                sc.wait_ge(x1_turned, r + 1)
                act_(xTh[:, :, r * P:(r + 1) * P], bank[:, T_BANK[r]:T_BANK[r] + 2, :].rearrange("p a (k l) -> p (a k) l", l=P),
                     ACT.Copy).then_inc(x1h_ready, 1)

            def hidden_high(m):
                sc.wait_ge(hidden_ready, 2 * m + 2)
                act_(half_slot(xTh, m), hidden[:, 2 * m:2 * m + 2, :], ACT.Copy).then_inc(hh_ready, 1)

            def tap_two(i, b=GATE_BANK):
                for f in range(2):
                    sc.wait_ge(gate_ready, 2 * i + f + 1)
                    act_(cv[:, f, :], bank[:, b + f, :], ACT.Identity, scale=convp[:, bass.ds(2 * i + (2 * FT + f), 1)],
                         bias=convp[:, bass.ds(2 * i + (3 * FT + f), 1)]).then_inc(tap2, 1)

            def gate(i):
                for f in range(2):
                    sc.wait_ge(tap0, 2 * i + f + 1)
                    act_(act[:, f, :], cv[:, f, :], ACT.Silu).then_inc(gated, 1)

            def next_gate_high(i):
                sc.wait_ge(gate_ready, 2 * i + 2)
                high(ff_in[0], 16 * i + 32, raw[:, 2, :], wh[0])

            def next_value_high(i):
                sc.wait_ge(val_ready, 2 * i + 2)
                high(ff_in[1], 16 * i + 32, raw[:, 1, :], wh[1])

            def up_step(i):
                gate(i)
                next_gate_high(i)
                sc.wait_ge(gated, 2 * i + 2)
                next_value_high(i)

            high(ff_in[1], 32, raw[:, 1, :], wh[1])
            tap_two(0)
            gate(0)
            sc.wait_ge(gated, 2)
            tap_two(1, SECOND_BANK)
            up_step(1)
            hidden_high(0)
            tap_two(2)
            with sc.Fori(2, UP_STEPS - 1) as i:
                up_step(i)
                tap_two(i + 1)
            next_gate_high(UP_STEPS - 1)
            gate(UP_STEPS - 1)
            next_value_high(UP_STEPS - 1)
            hidden_high(1)
            for m in range(2, DOWN):
                used = {DOWN_LOOP: None, 7: 5, 8: 4, 9: 5, 10: 6}.get(m, m - 2)
                if used is not None:
                    sc.wait_ge(down_used, used + 1)
                high(ff_in[m % 2], 16 * (UP_STEPS + m // 2 + 1), raw[:, 2 - m % 2, :], wh[down_slot(m)])
                hidden_high(m)

        @block.vector
        def _(dv):
            tt, ts_, stt = nc.vector.tensor_tensor, nc.vector.tensor_scalar, nc.vector.scalar_tensor_tensor

            def low(count, src, hi, dst):
                dv.wait_ge(high_ready, count)
                tt(dst[:, :], src, hi[:, :].bitcast(F32), ALU.subtract).then_inc(low_ready, 1)

            def low_qkv(c, pair):
                low(pair * NC + c + 1, raw[:, c % 3, :], wh[c % 3], wl[c % 3])

            nc.vector.memset(zeros[:, :], 0.0).then_inc(zeros_ready, 1)
            first = KT // 2 * CW
            dv.wait_ge(first_high, 1)
            tt(wl[0][:, 0:first], raw[:, 0, 0:first], wh[0][:, 0:first].bitcast(F32), ALU.subtract).then_inc(first_low, 1)
            for k in range(KT):
                dv.wait_ge(xh_ready, k + 1)
                tt(xTl[:, k, :], bank[:, k, :], xTh[:, k, :].bitcast(F32), ALU.subtract).then_inc(xl_ready, 1)
                if k == 2:
                    dv.wait_ge(high_ready, 1)
                    tt(wl[0][:, first:], raw[:, 0, first:], wh[0][:, first:].bitcast(F32), ALU.subtract).then_inc(low_ready, 1)
            low_qkv(1, 0)
            low_qkv(2, 0)
            dv.wait_ge(const_in_s, 16)
            dv.wait_ge(conv_ready, 1)

            def rope(c, pair, heads=(0, 1)):
                g, j = CHUNKS[c]
                for hh in heads:
                    t = 2 * c + hh
                    b = bank[:, t % 3, :]
                    dv.wait_ge(qk_tile, pair * QT + t + 1)
                    if t >= 2:
                        dv.wait_ge(rotated, pair * QT + t - 1)
                    by_cos, bc, cc = qk[:, g % 2, j, hh:hh + 1, :], bank[:, t % 3:t % 3 + 1, :], cosT.rearrange("p (o n) -> p o n", o=1)
                    if g > 0:
                        by_cos, bc, cc = tiles(by_cos), natural(bc), natural(cc)
                    tt(by_cos, bc, cc, ALU.mult)
                    tt(swapped[64:128, hh, :], b[0:64, :], sinT[0:64, :], ALU.mult)
                    tt(swapped[0:64, hh, :], b[64:128, :], sinT[64:128, :], ALU.mult).then_inc(rope_terms, 1)

            def mask(source, pair):
                for hh in range(2):
                    u = 2 * source + hh
                    dv.wait_ge(scores_ready, pair * 4 + u + 1)
                    ps = bank[:, SB + 2 * hh:SB + 2 * hh + 2, :].rearrange("p a (c k) -> p (a c) k", k=CW)
                    m = maskT[:, source:source + 1, :]
                    t0 = 1 - source
                    if source == 0:
                        stt(prob[:, u, 0, P:], ps[:, 0, P:], SCALE, maskT[:, 0, P:], ALU.mult, ALU.add)
                    stt(prob[:, u, t0:, :], ps[:, t0:, :], SCALE, m.broadcast_to([P, 4 - t0, CW]), ALU.mult, ALU.add).then_inc(masked, 1)
                for hh in range(2):
                    u = 2 * source + hh
                    c = 4 * hh
                    t0 = 1 - source
                    dv.wait_ge(masked, pair * 4 + u + 1)
                    if source == 0:
                        nc.vector.tensor_reduce(stats[:, 0, source, 0, c:c + 1], prob[:, u, 0, P:], X, ALU.max, negate=True)
                    nc.vector.tensor_reduce(stats[:, 0, source, 0, c + t0:c + 4], prob[:, u, t0:, :], X, ALU.max, negate=True).then_inc(shift_ready, 1)

            def spread_stats(pair):
                dv.wait_ge(probs_ready, pair * 4 + 4)
                own = stats[:, 0, :, :, :].rearrange("p s a (h o t) -> p (s a h) o t", h=2, o=1)
                tt(spread[:, :, :, :], own.broadcast_to([P, 8, NR, NR]), splitT.broadcast_to([P, 8, NR, NR]),
                   ALU.mult).then_inc(spread_ready, 1)

            def merge_sources(pair):
                step = [0]

                def link(ins):
                    step[0] += 1
                    ins.then_inc(merge_step, 1)
                    dv.wait_ge(merge_step, pair * 7 + step[0])

                dv.wait_ge(stats_sent, pair + 1)
                ex = bank[:, OB, 0:P].rearrange("p (s x t) -> p s x t", s=2, t=NR)
                link(tt(picked[:, :, :].rearrange("p (s x) t -> p s x t", s=2), ex, selT.broadcast_to([P, 2, 16, NR]), ALU.mult))
                link(nc.vector.tensor_reduce(stats[:, 1, :, :, :].rearrange("p s a c -> p (s a c)"), picked[:, :, :], X, ALU.add))
                link(tt(merge[:, 0, :, :], stats[:, 0, :, 0, :], stats[:, 1, :, 0, :], ALU.min))
                link(tt(merge[:, 1:3, :, :], merge[:, 0:1, :, :].broadcast_to([P, 2, 2, 8]), stats[:, :, :, 0, :], ALU.subtract))
                dv.wait_ge(mweight_ready, pair + 1)
                link(tt(merge[:, 3:5, :, :], mweight[:, :, :, :], stats[:, :, :, 1, :], ALU.mult))
                link(tt(merge[:, 0, :, :], merge[:, 3, :, :], merge[:, 4, :, :], ALU.add))
                link(nc.vector.reciprocal(merge[:, 3, :, :], merge[:, 0, :, :]))
                tt(coef[:, :, :], mweight[:, 0, :, :], merge[:, 3, :, :], ALU.mult).then_inc(coef_ready, 1)

            def scale(pair):
                dv.wait_ge(coef_ready, pair + 1)
                for source, hh in ((0, 0), (1, 0), (0, 1), (1, 1)):
                    u = 2 * source + hh
                    for t in range(4):
                        lo = P if source == 0 and t == 0 else 0
                        c = 4 * hh + t
                        last = ts_(prob[:, u, t, lo:], prob[:, u, t, lo:], coef[:, source, c:c + 1], None, ALU.mult)
                    last.then_inc(scaled, 1)

            rope(0, 0)
            low_qkv(3, 0)

            def attend(pair, last_pair):
                rope(1, pair)
                low_qkv(4, pair)
                rope(2, pair)
                low_qkv(5, pair)
                mask(0, pair)
                for c in range(3, 6):
                    rope(c, pair)
                    low_qkv(c + 3, pair)
                low_qkv(9, pair)
                mask(1, pair)
                spread_stats(pair)
                low_qkv(10, pair)
                merge_sources(pair)
                scale(pair)
                def store_turned(n, source):
                    dv.wait_ge(turned, pair * 4 + n + 1)
                    if n >= 2:
                        dv.wait_ge(summed, pair * 4 + n - 1)
                    w = S if source else 3 * P
                    nc.vector.tensor_copy(probT[:, source, S:S + w], bank[:, SB + 2 * source + 1, 0:w]).then_inc(turned_dve, 1)

                store_turned(0, 0)
                store_turned(1, 1)
                low_qkv(11, pair)
                if not last_pair:
                    rope(0, pair + 1, (0,))
                store_turned(2, 0)
                store_turned(3, 1)
                head(0, pair)
                if last_pair:
                    low(UP0, raw[:, 0, :], wh[3], wl[3])
                else:
                    rope(0, pair + 1, (1,))
                    low_qkv(12, pair)
                head(1, pair)

            def head(hh, pair):
                dv.wait_ge(head_high, pair * 2 + hh + 1)
                h = bass.ds(2 * pair + hh, 1)
                tt(oTl[:, h, :], bank[:, OB:OB + 1, :], oTh[:, h, :].bitcast(F32), ALU.subtract).then_inc(head_low, 1)

            with dv.Fori(0, PAIRS - 1) as pair:
                attend(pair, False)
            attend(PAIRS - 1, True)

            def layer_norm(i, r):
                n = NR * i + r
                b = (Y_BANK[r], 2 * r)[i]
                halves = [slice(0, S), slice(S, D)]
                if n >= 1:
                    dv.wait_ge(ln_done, 2 * n)
                for half, hs in enumerate(halves):
                    if n == 2 * NR - 1 and half == 0:
                        dv.wait_ge(y_half, 1)
                    else:
                        dv.wait_ge(y_ready, n + 1)
                    stt(zrow[:, hs], res[:, r, hs], ALPHA, bank[:, b + half, :], ALU.mult, ALU.add).then_inc(z_ready, 1)
                    if n == 2 * NR - 1 and half == 0:
                        dv.wait_ge(z_ready, 2 * n + 1)
                        nc.vector.bn_stats(small[:, 0:6], zrow[:, hs])
                for half, hs in enumerate(halves):
                    if n == 2 * NR - 1 and half == 0:
                        continue
                    dv.wait_ge(z_ready, 2 * n + 1 + half)
                    last = nc.vector.bn_stats(small[:, 6 * half:6 * half + 6], zrow[:, hs])
                last.then_inc(ln_stats, 1)
                dv.wait_ge(ln_stats, 3 * n + 1)
                nc.vector.bn_aggr(small[:, 12:14], small[:, 0:12]).then_inc(ln_stats, 1)
                dv.wait_ge(ln_stats, 3 * n + 2)
                nc.vector.tensor_scalar_add(small[:, 13:14], small[:, 13:14], EPS).then_inc(ln_stats, 1)
                if r == 0:
                    dv.wait_ge(ln_in, 32 * i + 32)
                for hs in halves:
                    stt(zrow[:, hs], zrow[:, hs], small[:, 12:13], lnp[:, 0, hs], ALU.subtract, ALU.mult).then_inc(centred, 1)
                dv.wait_ge(rstd_ready, n + 1)
                for half, hs in enumerate(halves):
                    dv.wait_ge(centred, 2 * n + half + 1)
                    stt(res[:, r, hs], zrow[:, hs], small[:, 14:15], lnp[:, 1, hs], ALU.mult, ALU.add).then_inc(ln_done, 1)

            def x1_low(r):
                ts = slice(r * P, (r + 1) * P)
                dv.wait_ge(x1h_ready, r + 1)
                tt(xTl[:, :, ts], bank[:, T_BANK[r]:T_BANK[r] + 2, :].rearrange("p a (k l) -> p (a k) l", l=P), xTh[:, :, ts].bitcast(F32),
                   ALU.subtract).then_inc(x1l_ready, 1)

            dv.wait_ge(res_in, 16)
            for r in range(NR):
                layer_norm(0, r)
                if 1 <= r < NR - 1:
                    x1_low(r - 1)
                if r == NR - 2:
                    low(UP0 + 1, raw[:, 2, :], wh[2], wl[2])
                    x1_low(r)
                    low(UP0 + 2, raw[:, 1, :], wh[3], wl[3])
            low(UP0 + 3, raw[:, 2, :], wh[0], wl[0])
            x1_low(NR - 1)
            low(UP0 + 4, raw[:, 1, :], wh[1], wl[1])

            def up_step(i, split=True, b=GATE_BANK):
                for f in range(2):
                    dv.wait_ge(tap2, 2 * i + f + 1)
                    stt(cv[:, f, 1:], bank[:, b + f, 0:S - 1], convp[:, bass.ds(2 * i + (FT + f), 1)], cv[:, f, 1:],
                        ALU.mult, ALU.add).then_inc(tap1, 1)
                for f in range(2):
                    dv.wait_ge(tap1, 2 * i + f + 1)
                    stt(cv[:, f, 2:], bank[:, b + f, 0:S - 2], convp[:, bass.ds(2 * i + f, 1)], cv[:, f, 2:],
                        ALU.mult, ALU.add).then_inc(tap0, 1)
                if split:
                    low(2 * i + UP0 + 3, raw[:, 2, :], wh[0], wl[0])
                for f in range(2):
                    dv.wait_ge(gated, 2 * i + f + 1)
                    dv.wait_ge(val_ready, 2 * i + f + 1)
                    tt(hidden[:, bass.ds(2 * i + f, 1), :], act[:, f:f + 1, :], bank[:, VAL_BANK + f:VAL_BANK + f + 1, :],
                       ALU.mult).then_inc(hidden_ready, 1)
                if split:
                    low(2 * i + UP0 + 4, raw[:, 1, :], wh[1], wl[1])

            def hidden_low(m):
                dv.wait_ge(hh_ready, m + 1)
                tt(half_slot(xTl, m), hidden[:, 2 * m:2 * m + 2, :], half_slot(xTh, m).bitcast(F32), ALU.subtract).then_inc(hl_ready, 1)

            up_step(0, False)
            up_step(1, b=SECOND_BANK)
            hidden_low(0)
            with dv.Fori(2, UP_STEPS - 1) as i:
                up_step(i)
            up_step(UP_STEPS - 1)
            hidden_low(1)
            for m in range(2, DOWN):
                s = down_slot(m)
                low(DOWN0 + m + 1, raw[:, 2 - m % 2, :], wh[s], wl[s])
                hidden_low(m)
            for r in range(NR):
                layer_norm(1, r)

        @block.gpsimd
        def _(pool):
            def add_terms(c, pair):
                g, j = CHUNKS[c]
                for hh in range(2):
                    pool.wait_ge(rope_terms, pair * QT + 2 * c + hh + 1)
                    a, b = qk[:, g % 2, j, hh:hh + 1, :], swapped[:, hh:hh + 1, :]
                    if g > 0:
                        a, b = tiles(a), natural(b)
                    nc.gpsimd.tensor_tensor(a, a, b, ALU.add).then_inc(rotated, 1)

            nc.gpsimd.memset(small[:, 16:17], -0.5).then_inc(exponent, 1)
            add_terms(0, 0)

            def attend(pair, last_pair):
                for c in range(1, 6):
                    add_terms(c, pair)
                if not last_pair:
                    add_terms(0, pair + 1)

            with pool.Fori(0, PAIRS - 1) as pair:
                attend(pair, False)
            attend(PAIRS - 1, True)

            pool.wait_ge(exponent, 1)
            for n in range(2 * NR):
                pool.wait_ge(ln_stats, 3 * n + 3)
                nc.gpsimd.tensor_tensor(small[:, 14:15], small[:, 13:14], small[:, 16:17], ALU.pow).then_inc(rstd_ready, 1)


def kernel(x, attn_w_in, attn_w_out, ffn_w_up, ffn_conv_w, ffn_conv_b, ffn_w_down, ln_g, ln_b, **unused):
    import concourse.bacc as bacc
    from concourse.bass_utils import run_bass_kernel_spmd

    nc = bacc.Bacc("TRN2", target_bir_lowering=False, num_devices=1)
    arrays = {
        "x": x, "w_in": attn_w_in, "w_out": attn_w_out, "w_up": ffn_w_up, "conv_w": ffn_conv_w,
        "conv_b": ffn_conv_b, "w_down": ffn_w_down, "ln_g": ln_g, "ln_b": ln_b,
        "ident": np.eye(P, dtype=np.float32), "const": constants(),
    }
    arrays = {n: np.ascontiguousarray(a) for n, a in arrays.items()}
    args = [nc.dram_tensor(f"in_{n}", a.shape, F32, kind="ExternalInput").ap() for n, a in arrays.items()]
    out = nc.dram_tensor("out", (1, S, D), F32, kind="ExternalOutput").ap()
    layer(nc, *args, out)
    r = run_bass_kernel_spmd(nc, [{f"in_{n}": a for n, a in arrays.items()}], core_ids=[0])
    return r.results[0]["out"]
```
